# Optimizing a Trainium2 kernel written in Bass

```python
import math
import jax
import jax.numpy as jnp
from jax import lax
import numpy as np

D_MODEL = 1024
BATCH = 1
SEQ = 512
DEPTH = 1

HEAD_DIM = 64
ATTN_GROUPS = ((128, 1), (512, 4), (2048, 16))
HEADS_PER_GROUP = 8
N_ATTN_HEADS = HEADS_PER_GROUP * len(ATTN_GROUPS)
ATTN_WIDTH = N_ATTN_HEADS * HEAD_DIM
ATTN_OUT_WIDTH = HEADS_PER_GROUP * HEAD_DIM
BLOCK = 128
NUM_BUCKETS = 32
MAX_DISTANCE = 2048

D_INNER = 2 * D_MODEL
SSM_HEAD_DIM = 64
N_SSM_HEADS = D_INNER // SSM_HEAD_DIM
N_SSM_GROUPS = 4
D_STATE = 128
CONV_WIDTH = 4
CHUNK = 128
CONV_DIM = D_INNER + 2 * N_SSM_GROUPS * D_STATE

N_BRANCHES = 2
SPLIT_POINTS = (ATTN_WIDTH, 2 * ATTN_WIDTH, 3 * ATTN_WIDTH,
                3 * ATTN_WIDTH + D_INNER,
                3 * ATTN_WIDTH + D_INNER + CONV_DIM,
                3 * ATTN_WIDTH + D_INNER + CONV_DIM + N_SSM_HEADS)
IN_PROJ_WIDTH = 3 * ATTN_WIDTH + D_INNER + CONV_DIM + N_SSM_HEADS + N_BRANCHES * D_MODEL

N_EXPERTS = 32
TOP_K = 4
D_EXPERT = D_MODEL
SWIGLU_LIMIT = 7.0
SWIGLU_ALPHA = 1.702
MOE_BLOCK = 128

EPS = 1e-5

kernel_name = 'hybrid_dilated_attn_ssd_moe'

def rmsnorm(x, w):
    xf = x.astype(jnp.float32)
    y = xf * lax.rsqrt(jnp.mean(xf * xf, axis=-1, keepdims=True) + EPS)
    return (y * w.astype(jnp.float32)).astype(x.dtype)

def t5_bucket(dist):
    max_exact = NUM_BUCKETS // 2
    nf = jnp.maximum(dist, max_exact).astype(jnp.float32)
    large = max_exact + (jnp.log(nf / max_exact) / math.log(MAX_DISTANCE / max_exact)
                         * (NUM_BUCKETS - max_exact)).astype(jnp.int32)
    large = jnp.minimum(large, NUM_BUCKETS - 1)
    return jnp.where(dist < max_exact, dist, large)

def dilated_window_attention(q, k, v, bias_table, window, dilation):
    b, s, h, hd = q.shape
    span = dilation * BLOCK
    s_pad = -(-s // span) * span
    sub_len = s_pad // dilation
    nb = sub_len // BLOCK
    w_sub = window // dilation

    def to_sub(t):
        t = jnp.pad(t.astype(jnp.float32), ((0, 0), (0, s_pad - s), (0, 0), (0, 0)))
        t = t.reshape(b, sub_len, dilation, h, hd).transpose(0, 2, 1, 3, 4)
        return t.reshape(b * dilation, nb, BLOCK, h, hd)

    def with_prev(t):
        prev = jnp.pad(t, ((0, 0), (1, 0), (0, 0), (0, 0), (0, 0)))[:, :-1]
        return jnp.concatenate([prev, t], axis=2)

    qb = to_sub(q)
    kc = with_prev(to_sub(k))
    vc = with_prev(to_sub(v))
    logits = jnp.einsum('znqhd,znkhd->znhqk', qb, kc) * (hd ** -0.5)
    q_idx = jnp.arange(BLOCK)[:, None]
    k_idx = jnp.arange(2 * BLOCK)[None, :]
    delta = q_idx + BLOCK - k_idx
    in_band = (delta >= 0) & (delta <= w_sub)
    has_prev = (jnp.arange(nb)[:, None, None] > 0) | (k_idx >= BLOCK)[None]
    valid = in_band[None] & has_prev
    bucket = t5_bucket(jnp.clip(delta, 0, w_sub) * dilation)
    bias = jnp.transpose(bias_table.astype(jnp.float32)[bucket], (2, 0, 1))
    logits = jnp.where(valid[None, :, None], logits + bias[None, None], -jnp.inf)
    m = jnp.max(logits, axis=-1, keepdims=True)
    p = jnp.exp(logits - m)
    denom = jnp.sum(p, axis=-1, keepdims=True)
    lse = (m + jnp.log(denom))[..., 0]
    out = jnp.einsum('znhqk,znkhd->znqhd', p / denom, vc)
    out = out.reshape(b, dilation, sub_len, h, hd).transpose(0, 2, 1, 3, 4).reshape(b, s_pad, h, hd)[:, :s]
    lse = lse.transpose(0, 1, 3, 2).reshape(b, dilation, sub_len, h).transpose(0, 2, 1, 3).reshape(b, s_pad, h)[:, :s]
    return out, lse

def causal_depthwise_conv(u, w, bias):
    c = u.shape[-1]
    out = lax.conv_general_dilated(u, w[:, None, :].astype(u.dtype), window_strides=(1,),
                                   padding=[(CONV_WIDTH - 1, 0)],
                                   dimension_numbers=('NWC', 'WIO', 'NWC'),
                                   feature_group_count=c)
    return out + bias.astype(u.dtype)

def ssd_chunked(xs, dt, a, bm, cm):
    b, s, h, p = xs.shape
    g, n = bm.shape[2], bm.shape[3]
    r = h // g
    nc = s // CHUNK
    x_d = (xs * dt[..., None]).reshape(b, nc, CHUNK, g, r, p)
    a_d = jnp.moveaxis((dt * a).reshape(b, nc, CHUNK, g, r), 2, -1)
    a_cs = jnp.cumsum(a_d, axis=-1)
    bc = bm.reshape(b, nc, CHUNK, g, n)
    cc = cm.reshape(b, nc, CHUNK, g, n)
    tril = jnp.tril(jnp.ones((CHUNK, CHUNK), dtype=bool))
    seg = a_cs[..., :, None] - a_cs[..., None, :]
    decay_in = jnp.exp(jnp.where(tril, seg, -jnp.inf))
    cb = jnp.einsum('bclgn,bcsgn->bcgls', cc, bc)
    y_diag = jnp.einsum('bcgrls,bcsgrp->bclgrp', cb[:, :, :, None] * decay_in, x_d)
    decay_states = jnp.exp(a_cs[..., -1:] - a_cs)
    states = jnp.einsum('bclgn,bcgrl,bclgrp->bcgrpn', bc, decay_states, x_d)
    chunk_decay = jnp.exp(a_cs[..., -1])

    def step(carry, inp):
        st, dec = inp
        return carry * dec[..., None, None] + st, carry

    init = jnp.zeros((b, g, r, p, n), jnp.float32)
    _, prev = lax.scan(step, init, (jnp.moveaxis(states, 1, 0), jnp.moveaxis(chunk_decay, 1, 0)))
    prev = jnp.moveaxis(prev, 0, 1)
    y_off = jnp.einsum('bclgn,bcgrpn,bcgrl->bclgrp', cc, prev, jnp.exp(a_cs))
    return (y_diag + y_off).reshape(b, s, h, p)

def hybrid_mixer(h, w_in, rel_bias, w_branch_attn, conv_w, conv_b, dt_bias, a_log, d_skip,
                 ssm_norm_w, w_branch_ssm, gate_bias, w_out):
    b, s, _ = h.shape
    f32 = jnp.float32
    proj = h @ w_in
    q, k, v, z, xbc, dt_raw, gate_logits = jnp.split(proj, SPLIT_POINTS, axis=-1)

    q = q.reshape(b, s, N_ATTN_HEADS, HEAD_DIM)
    k = k.reshape(b, s, N_ATTN_HEADS, HEAD_DIM)
    v = v.reshape(b, s, N_ATTN_HEADS, HEAD_DIM)
    outs, lses = [], []
    for gi, (window, dilation) in enumerate(ATTN_GROUPS):
        hs = slice(gi * HEADS_PER_GROUP, (gi + 1) * HEADS_PER_GROUP)
        o, l = dilated_window_attention(q[:, :, hs], k[:, :, hs], v[:, :, hs], rel_bias[:, hs], window, dilation)
        outs.append(o)
        lses.append(l)
    mix_w = jax.nn.softmax(jnp.stack(lses, axis=0), axis=0)
    attn = jnp.sum(mix_w[..., None] * jnp.stack(outs, axis=0), axis=0).reshape(b, s, ATTN_OUT_WIDTH)
    y_attn = attn.astype(h.dtype) @ w_branch_attn

    xbc = jax.nn.silu(causal_depthwise_conv(xbc, conv_w, conv_b))
    xs, bm, cm = jnp.split(xbc, [D_INNER, D_INNER + N_SSM_GROUPS * D_STATE], axis=-1)
    xs = xs.reshape(b, s, N_SSM_HEADS, SSM_HEAD_DIM).astype(f32)
    bm = bm.reshape(b, s, N_SSM_GROUPS, D_STATE).astype(f32)
    cm = cm.reshape(b, s, N_SSM_GROUPS, D_STATE).astype(f32)
    dt = jax.nn.softplus(dt_raw.astype(f32) + dt_bias.astype(f32))
    a = -jnp.exp(a_log.astype(f32))
    y = ssd_chunked(xs, dt, a, bm, cm) + d_skip.astype(f32)[:, None] * xs
    y = y.reshape(b, s, D_INNER) * jax.nn.silu(z.astype(f32))
    yg = y.reshape(b, s, N_SSM_GROUPS, D_INNER // N_SSM_GROUPS)
    yg = yg * lax.rsqrt(jnp.mean(yg * yg, axis=-1, keepdims=True) + EPS)
    y = yg.reshape(b, s, D_INNER) * ssm_norm_w.astype(f32)
    y_ssm = y.astype(h.dtype) @ w_branch_ssm

    gates = jax.nn.sigmoid((gate_logits + gate_bias).astype(f32)).reshape(b, s, N_BRANCHES, D_MODEL)
    merged = gates[..., 0, :] * y_attn.astype(f32) + gates[..., 1, :] * y_ssm.astype(f32)
    return merged.astype(h.dtype) @ w_out

def clamped_swiglu(hid):
    x_glu = jnp.minimum(hid[..., ::2], SWIGLU_LIMIT)
    x_lin = jnp.clip(hid[..., 1::2], -SWIGLU_LIMIT, SWIGLU_LIMIT)
    return x_glu * jax.nn.sigmoid(SWIGLU_ALPHA * x_glu) * (x_lin + 1.0)

def moe_ffn(h, router_w, router_b, w1, b1, w2, b2):
    b, s, d = h.shape
    t_n = b * s
    tok = h.reshape(t_n, d)
    logits = (tok @ router_w + router_b).astype(jnp.float32)
    top_val, top_idx = lax.top_k(logits, TOP_K)
    weights = jax.nn.softmax(top_val, axis=-1)
    n_assign = t_n * TOP_K
    flat_e = top_idx.reshape(n_assign)
    flat_tok = jnp.arange(n_assign, dtype=jnp.int32) // TOP_K
    flat_w = weights.reshape(n_assign)
    order = jnp.argsort(flat_e)
    se, stok, sw = flat_e[order], flat_tok[order], flat_w[order]
    counts = jnp.bincount(flat_e, length=N_EXPERTS)
    padded = (counts + MOE_BLOCK - 1) // MOE_BLOCK * MOE_BLOCK
    start = jnp.cumsum(counts) - counts
    pend = jnp.cumsum(padded)
    pstart = pend - padded
    dest = pstart[se] + jnp.arange(n_assign, dtype=jnp.int32) - start[se]
    cap = n_assign + N_EXPERTS * MOE_BLOCK
    n_blocks = cap // MOE_BLOCK
    buf = jnp.zeros((cap, d), h.dtype).at[dest].set(tok[stok])
    block_e = jnp.minimum(jnp.searchsorted(pend, jnp.arange(n_blocks) * MOE_BLOCK, side='right'), N_EXPERTS - 1)

    def expert_block(args):
        xb, e = args
        hid = xb @ w1[e] + b1[e]
        return clamped_swiglu(hid) @ w2[e] + b2[e]

    ybuf = lax.map(expert_block, (buf.reshape(n_blocks, MOE_BLOCK, d), block_e)).reshape(cap, d)
    y = ybuf[dest] * sw[:, None].astype(ybuf.dtype)
    out = jax.ops.segment_sum(y, stok, num_segments=t_n)
    return out.reshape(b, s, d)

def setup_inputs(seed: int = 0) -> dict:
    key = jax.random.key(seed)
    ks = jax.random.split(key, 24)
    f32 = jnp.float32

    def nrm(k, shape, scale):
        return jax.random.normal(k, shape, f32) * scale

    dt0 = jnp.exp(jax.random.uniform(ks[6], (DEPTH, N_SSM_HEADS), f32, math.log(1e-3), math.log(1e-1)))
    return {
        'x': nrm(ks[0], (BATCH, SEQ, D_MODEL), 1.0),
        'w_in': nrm(ks[1], (DEPTH, D_MODEL, IN_PROJ_WIDTH), D_MODEL ** -0.5),
        'rel_bias': nrm(ks[2], (NUM_BUCKETS, N_ATTN_HEADS), 0.5),
        'w_branch_attn': nrm(ks[3], (DEPTH, ATTN_OUT_WIDTH, D_MODEL), ATTN_OUT_WIDTH ** -0.5),
        'conv_w': nrm(ks[4], (DEPTH, CONV_WIDTH, CONV_DIM), CONV_WIDTH ** -0.5),
        'conv_b': nrm(ks[5], (DEPTH, CONV_DIM), 0.02),
        'dt_bias': dt0 + jnp.log(-jnp.expm1(-dt0)),
        'a_log': jnp.log(jax.random.uniform(ks[7], (DEPTH, N_SSM_HEADS), f32, 1.0, 16.0)),
        'd_skip': 1.0 + nrm(ks[8], (DEPTH, N_SSM_HEADS), 0.1),
        'ssm_norm_w': 1.0 + nrm(ks[9], (DEPTH, D_INNER), 0.1),
        'w_branch_ssm': nrm(ks[10], (DEPTH, D_INNER, D_MODEL), D_INNER ** -0.5),
        'gate_bias': nrm(ks[11], (DEPTH, N_BRANCHES * D_MODEL), 0.1),
        'w_out': nrm(ks[12], (DEPTH, D_MODEL, D_MODEL), D_MODEL ** -0.5),
        'norm_mix': 1.0 + nrm(ks[13], (DEPTH, D_MODEL), 0.1),
        'norm_ffn': 1.0 + nrm(ks[14], (DEPTH, D_MODEL), 0.1),
        'router_w': nrm(ks[15], (DEPTH, D_MODEL, N_EXPERTS), D_MODEL ** -0.5),
        'router_b': nrm(ks[16], (DEPTH, N_EXPERTS), 0.01),
        'w1': nrm(ks[17], (DEPTH, N_EXPERTS, D_MODEL, 2 * D_EXPERT), D_MODEL ** -0.5),
        'b1': nrm(ks[18], (DEPTH, N_EXPERTS, 2 * D_EXPERT), 0.01),
        'w2': nrm(ks[19], (DEPTH, N_EXPERTS, D_EXPERT, D_MODEL), D_EXPERT ** -0.5),
        'b2': nrm(ks[20], (DEPTH, N_EXPERTS, D_MODEL), 0.01),
        'norm_final': 1.0 + nrm(ks[21], (D_MODEL,), 0.1),
    }

def reference(x, w_in, rel_bias, w_branch_attn, conv_w, conv_b, dt_bias, a_log, d_skip, ssm_norm_w,
              w_branch_ssm, gate_bias, w_out, norm_mix, norm_ffn, router_w, router_b, w1, b1, w2, b2,
              norm_final):
    for l in range(DEPTH):
        h = rmsnorm(x, norm_mix[l])
        x = x + hybrid_mixer(h, w_in[l], rel_bias, w_branch_attn[l], conv_w[l], conv_b[l], dt_bias[l],
                             a_log[l], d_skip[l], ssm_norm_w[l], w_branch_ssm[l], gate_bias[l], w_out[l])
        h = rmsnorm(x, norm_ffn[l])
        x = x + moe_ffn(h, router_w[l], router_b[l], w1[l], b1[l], w2[l], b2[l])
    return rmsnorm(x, norm_final)


_drawn_inputs = setup_inputs


def setup_inputs(seed=0):
    import zlib

    import numpy as np

    out = dict(_drawn_inputs(seed))
    spreads = {}
    factors = {'b1': 8.0, 'b2': 8.0}
    for name, (base, spread) in spreads.items():
        noise = np.random.default_rng([zlib.crc32(name.encode()), seed]).standard_normal(out[name].shape)
        drawn = base * np.exp(spread * noise) if base else spread * noise
        out[name] = jnp.asarray(drawn.astype(out[name].dtype))
    for name, factor in factors.items():
        out[name] = (out[name] * factor).astype(out[name].dtype)
    return out
```

```python
from contextlib import ExitStack

import concourse.bass as bass
from concourse import mybir

F32 = mybir.dt.float32
F32R = mybir.dt.float32r
BF16 = mybir.dt.bfloat16
I32 = mybir.dt.int32
U32 = mybir.dt.uint32
ALU = mybir.AluOpType
ACT = mybir.ActivationFunctionType
AX = mybir.AxisListType

P = 128
SEQ, D = 512, 1024
TT = SEQ // P
KD = D // P
EPS = 1e-5
NE, TOPK = 32, 4
HID = 2 * D
CAP = 128
NPASS = SEQ // CAP
BIG = 1e30

RING = 4
GW = 2048
MIX_GRANULES = 60
STEPS = 4 * NE
PASS_GRANULES = 3 * STEPS

ARENA = 15488

C_ID, C_LE, C_GT, C_ONE, C_END = 0, 128, 256, 384, 512
C_LT, C_IOTA, C_ALL = 512, 640, 672

NG, HPG, HEAD_DIM = 3, 8, 64
NH_A, NHS, NSG = 24, 32, 4
CONV_WIDTH = 4
GROUPS = ((128, 1), (512, 4), (2048, 16))
NBK, MAX_DIST = 32, 2048
BR = 384
SKEW = P * (BR + 1)
COL_Z = 3 * NH_A * HEAD_DIM
COL_X = COL_Z + 2 * D
COL_B = COL_X + 2 * D
COL_DT = COL_B + 2 * 512
COL_G = COL_DT + NHS


def bc(ap, pairs):
    return bass.AP(ap.tensor, ap.offset, [list(ap.ap[0])] + [list(q) for q in pairs])


class Tally:

    def __init__(self, eng, sem):
        self.eng, self.sem, self.n = eng, sem, 0

    def __call__(self, ins):
        ins.then_inc(self.sem, 1)
        self.n += 1
        self.eng.wait_ge(self.sem, self.n)


def build(nc, x, w_in, rel_bias, w_branch_attn, conv_w, conv_b, dt_bias, a_log, d_skip, ssm_norm_w,
          w_branch_ssm, gate_bias, w_out, norm_mix, norm_ffn, router_w, router_b, w1, b1, w2, b2, norm_final, consts,
          buckets, out):
    with ExitStack() as ctx:
        def sb(name, shape, dt=F32):
            return ctx.enter_context(nc.sbuf_tensor(name, shape, dt))

        def sem(name):
            return ctx.enter_context(nc.semaphore(name))

        def dram(name, shape, dt=F32):
            return nc.dram_tensor(name, shape, dt, kind="Internal").ap()

        raw = sb("raw", [P, RING, GW])
        whi = sb("whi", [P, RING, GW], F32R)
        wlo = sb("wlo", [P, RING, GW], F32R)
        t_hi = sb("t_hi", [P, KD, SEQ], F32R)
        t_lo = sb("t_lo", [P, KD, SEQ], F32R)
        u_hi = sb("u_hi", [P, 4, SEQ], F32R)
        u_lo = sb("u_lo", [P, 4, SEQ], F32R)
        cst = sb("cst", [P, C_END])
        arena = sb("arena", [P, ARENA])
        bank = ctx.enter_context(nc.psum_tensor("bank", [P, 8, 512], F32))
        ident, tri_le, tri_gt = cst[:, C_ID:C_LE], cst[:, C_LE:C_GT], cst[:, C_GT:C_ONE]
        ones = cst[:, C_ONE:C_END]

        class Region:

            def __init__(self, first, end):
                self.at, self.end = first, end

            def __call__(self, *dims, dt=F32, parts=P):
                n = 1
                for d in dims:
                    n *= d
                words = n if dt != BF16 else (n + 1) // 2
                ap = arena[0:parts, self.at:self.at + words]
                self.at += words
                assert self.at <= self.end
                if dt != F32:
                    ap = ap.bitcast(dt)
                if len(dims) > 1:
                    names = "abcd"[:len(dims)]
                    ap = ap.rearrange(f"p ({' '.join(names)}) -> p {' '.join(names)}",
                                      **dict(zip(names[1:], dims[1:])))
                return ap

        keep = Region(0, 4096 + 960)
        resid = keep(TT, D)
        wk = keep(TT, TOPK)
        wk_pass = keep(NPASS, TT * TOPK)
        slot_i = keep(TT * TOPK, dt=I32)
        place_i = keep(TT * TOPK, dt=I32)
        tokc = keep(TT, dt=I32)
        flag_i = keep(1, dt=I32)
        idx = keep(1, dt=I32)
        ss, rstd, ss2, rstd2, wsum, wrec, longest = [keep(4) for _ in range(7)]
        table = keep(NPASS, NE, dt=I32)
        one3 = keep(P, dt=BF16, parts=3)
        route = Region(5056, ARENA)
        h2 = route(TT, D)
        h2t = route(KD, SEQ)
        wffn = h2t[:, 0:2].rearrange("p a b -> p (a b)")
        rw = route(KD, NE)
        rb = route(NE)
        logit = route(TT, NE)
        mx8 = route(TT, 8)
        ix8 = route(TT, 8, dt=U32)
        ixf = route(TT, TOPK)
        mask = route(TT, NE)
        hot = route(TT * TOPK, NE)
        hotr = route(TT * TOPK, NE)
        late = route(160)
        tri_lt, iota = late[:, 0:P], late[:, P:160]
        rk = route(4, TT * TOPK)
        addr = route(2, TT * TOPK)
        expert = Region(5056, ARENA)
        xg = expert(KD, P)
        ysb = expert(D)
        glu, lin, sig, prod = [expert(256) for _ in range(4)]
        act_t = [expert(256) for _ in range(2)]
        bias1 = [expert(1024, dt=BF16, parts=3) for _ in range(2)]
        bias2 = expert(1024, dt=BF16, parts=3)
        wfin = expert(D)
        h2_d = dram("h2_d", (SEQ, D))
        tok_d = dram("tok_d", (NPASS * P * NE, 1), I32)
        y_d = dram("y_d", (NE * P, D))
        bias_d = dram("bias_d", (NE, 3, 3072), BF16)

        raw_in = [sem(f"raw_in{s}") for s in range(RING)]
        hi_done, lo_done, granule_used = sem("hi_done"), sem("lo_done"), sem("granule_used")
        const_in, bias_raw_in, bias_split, bias_saved = (sem("const_in"), sem("bias_raw_in"),
                                                         sem("bias_split"), sem("bias_saved"))
        tok_zeroed, zero_set, ids_set = sem("tok_zeroed"), sem("zero_set"), sem("ids_set")
        x_in, sq_done, rms_ready, norm_in, h2_ready, h2_saved = (sem("x_in"), sem("sq_done"), sem("rms_ready"),
                                                       sem("norm_in"), sem("h2_ready"), sem("h2_saved"))
        h2t_psum, h2t_copied, logit_psum, router_in = (sem("h2t_psum"), sem("h2t_copied"),
                                                       sem("logit_psum"), sem("router_in"))
        top_found, exp_done, mask_ready, rank_psum = (sem("top_found"), sem("exp_done"), sem("mask_ready"),
                                                      sem("rank_psum"))
        places_ready, tok_saved, table_in, flag_ready = (sem("places_ready"), sem("tok_saved"),
                                                         sem("table_in"), sem("flag_ready"))
        idx_ready, xg_in, xt_psum, xt_hi, xt_lo = (sem("idx_ready"), sem("xg_in"), sem("xt_psum"), sem("xt_hi"),
                                                   sem("xt_lo"))
        bias1_in = [sem("bias1a_in"), sem("bias1b_in")]
        bias2_in = sem("bias2_in")
        h_done, glu_ready, lin_ready, sig_done, prod_ready, act_ready = (
            sem("h_done"), sem("glu_ready"), sem("lin_ready"), sem("sig_done"), sem("prod_ready"), sem("act_ready"))
        at_psum, at_hi, at_lo = sem("at_psum"), sem("at_hi"), sem("at_lo")
        y_done, y_copied, y_saved = sem("y_done"), sem("y_copied"), sem("y_saved")
        comb_in = [sem(f"comb_in{i}") for i in range(8)]
        comb_used = sem("comb_used")
        sq2_done, rms2_ready, fin_in, out_ready, out_saved = (
            sem("sq2_done"), sem("rms2_ready"), sem("fin_in"), sem("out_ready"),
            sem("out_saved"))
        dve_own = sem("dve_own")
        late_in, one3_set = sem("late_in"), sem("one3_set")

        x_t = Region(0, 4096)(TT, D)
        early = Region(4096, ARENA)
        hotb = early(3 * BR + NH_A, parts=NBK + 1)
        rowb = early(3, BR, parts=HPG)
        bfull = early(3072, parts=NE)
        bpart = early(3, 3072, dt=BF16, parts=NE)
        zero_i = early(P, dt=I32)
        ldrows = early(P)
        ldrows2 = early(P)
        dtw_raw = Region(0, 4096)(KD, NHS)
        att = Region(0, ARENA)
        q_t = [att(4, SEQ) for _ in range(NG)]
        k_t = att(4, SEQ)
        v_t = att(TT, 512)
        bias_t = att(HPG, 256)
        logit_t = att(TT, 256)
        prob_t = att(TT, 256)
        pturn = att(7, P)
        m_all = att(NG, TT, HPG)
        d_all = att(NG, TT, HPG)
        merge = Region(6144, ARENA)
        m_row = merge(NG, SEQ, parts=HPG)
        d_row = merge(NG, SEQ, parts=HPG)
        e_row = merge(NG, SEQ, parts=HPG)
        top_row = merge(SEQ, parts=HPG)
        z_row = merge(SEQ, parts=HPG)
        ssd = Region(0, ARENA)
        b_t = ssd(SEQ)
        c_t = ssd(SEQ)
        b_tok = ssd(TT, P)
        cbm = ssd(TT, P)
        xs = ssd(TT, 512)
        zs = ssd(TT, 512)
        conv_t = [ssd(SEQ) for _ in range(2)]
        ramp = ssd(HPG, P)
        dec = [ssd(HPG, P) for _ in range(2)]
        xd = [ssd(512) for _ in range(2)]
        xdd = ssd(512)
        skip = ssd(512)
        state = ssd(512)
        y_t = ssd(512)
        y_turn = [ssd(SEQ) for _ in range(2)]
        dts = ssd(TT, NHS)
        a_d = ssd(TT, NHS)
        dec3 = ssd(3, TT, NHS)
        dskip = ssd(NHS)
        a_neg = ssd(NHS)
        dtb = ssd(NHS)
        sp = [y_turn[0][:, i * 128:(i + 1) * 128].rearrange("p (t h) -> p t h", t=TT) for i in range(4)]
        gates = Region(4096, 4096 + 8192)(2, KD, SEQ)
        y_back = [Region(0, 2048)(4, SEQ), Region(2048, 4096)(4, SEQ), Region(12288, 14336)(4, SEQ)]
        small = sb("small", [P, 176])
        msm = small[:, 0:4], small[:, 4:8]
        ms, mrstd = msm
        nm_t = small[:, 8:12]
        gss, grstd = small[:, 12:16], small[:, 16:20]
        dt_raw = small[:, 20:148].rearrange("p (t h) -> p t h", t=TT)
        cols = sb("cols", [P, 160])
        col_cw = lambda j, f: cols[:, 24 * j + f:24 * j + f + 1]
        col_cb = lambda f: cols[:, 96 + f:97 + f]
        col_nm = lambda k: cols[:, 120 + k:121 + k]
        col_gb = lambda f: cols[:, 128 + f:129 + f]
        col_sn = lambda f: cols[:, 144 + f:145 + f]

        rel_d = dram("rel_d", (NG * HPG * SKEW, 1))
        yt_d = dram("yt_d", (NSG, 4, P, SEQ))

        cols_in, cols_psum, cols_ready = sem("cols_in"), sem("cols_psum"), sem("cols_ready")
        xm_in, msq_done, mrms, xn_ready, ht_psum, ht_hi, ht_lo = (
            sem("xm_in"), sem("msq_done"), sem("mrms"), sem("xn_ready"), sem("ht_psum"), sem("ht_hi"), sem("ht_lo"))
        buckets_in, table_rows_in, rel_psum, rel_copied, rel_saved, bias_in = (
            sem("buckets_in"), sem("table_rows_in"), sem("rel_psum"), sem("rel_copied"), sem("rel_saved"),
            sem("bias_in"))
        dtw_in, dtw_hi, dtw_lo, dt_psum, dt_out = (sem("dtw_in"), sem("dtw_hi"), sem("dtw_lo"), sem("dt_psum"),
                                                   sem("dt_out"))
        tile_done, act_out, dve_out = sem("tile_done"), sem("act_out"), sem("dve_out")
        s_psum, s_out, neg_ready, p_ready, pt_psum, pt_out, u_psum, u_out = (
            sem("s_psum"), sem("s_out"), sem("neg_ready"), sem("p_ready"), sem("pt_psum"), sem("pt_out"),
            sem("u_psum"), sem("u_out"))
        row_psum, row_out, row_less, row_exp, share_ready, share_psum, share_used = (
            sem("row_psum"), sem("row_out"), sem("row_less"), sem("row_exp"), sem("share_ready"),
            sem("share_psum"), sem("share_used"))
        attn_sum, attn_hi, attn_lo = sem("attn_sum"), sem("attn_hi"), sem("attn_lo")
        dtc_in, sp_abs, sp_exp, sp_one, sp_ln, a_ready, cs_psum, cs_exp = (
            sem("dtc_in"), sem("sp_abs"), sem("sp_exp"), sem("sp_one"), sem("sp_ln"), sem("a_ready"), sem("cs_psum"),
            sem("cs_exp"))
        conv_on, conv_silu = sem("conv_on"), sem("conv_silu")
        xs_psum, xs_out, bt_psum, bt_out, cb_psum, cb_out = (
            sem("xs_psum"), sem("xs_out"), sem("bt_psum"), sem("bt_out"), sem("cb_psum"), sem("cb_out"))
        ramp_ready, seg_psum, dec_ready, mat_ready, xd_ready, xdd_ready = (
            sem("ramp_ready"), sem("seg_psum"), sem("dec_ready"), sem("mat_ready"), sem("xd_ready"),
            sem("xdd_ready"))
        off_psum, st_psum, diag_psum, off_used, st_used, y_chunk = (
            sem("off_psum"), sem("st_psum"), sem("diag_psum"), sem("off_used"), sem("st_used"), 
            sem("y_chunk"))
        skip_ready, skip_used = sem("skip_ready"), sem("skip_used")
        gsq_done, grms, yn_ready, yt_psum, yt_out, yt_in = (
            sem("gsq_done"), sem("grms"), sem("yn_ready"), sem("yt_psum"), sem("yt_out"), sem("yt_in"))
        yt_saved = [sem("yt_saved0"), sem("yt_saved1")]
        yb_in = [sem(f"yb_in{i}") for i in range(3)]
        yb_hi, yb_lo = sem("yb_hi"), sem("yb_lo")
        merged_f, merged_hi, merged_lo = sem("merged_f"), sem("merged_hi"), sem("merged_lo")

        panels = []
        for g in range(NG):
            panels += [("q", g, 4, 2, "act"), ("k", g, 4, 2, "act"), ("v", g, 4, 2, "act")]
        for g in range(NSG):
            panels += [("bc", g, 2, 1, "dve"), ("xs", g, 4, 2, "dve"), ("z", g, 4, 2, "act")]
        panels += [("gate", i, 4, 2, "act") for i in range(4)]
        panels += [("attn", h, 4, 1, "dve") for h in range(2)]
        panels += [("ssm", 2 * g + h, 4, 1, "dve" if g == NSG - 1 else None) for g in range(NSG) for h in range(2)]
        panels += [("out", h, 4, 2, "dve") for h in range(2)]

        first_of, ready_at, out_at, landed_at = {}, {}, {}, {}
        n_granule, n_tile, n_out, n_slot = 0, 0, {"act": 0, "dve": 0, None: 0}, [0] * RING
        for name, g, tiles, granules, owner in panels:
            first_of[name, g] = n_granule
            for j in range(tiles):
                if j < tiles - 1:
                    n_tile += 1
                    ready_at[name, g, j] = (tile_done, n_tile)
                else:
                    ready_at[name, g, j] = (granule_used, n_granule + granules)
                n_out[owner] += 1
                out_at[name, g, j] = (act_out if owner == "act" else dve_out, n_out[owner])
            for _ in range(granules):
                n_slot[n_granule % RING] += 2 if name == "bc" else 1
                landed_at[n_granule] = 16 * n_slot[n_granule % RING]
                n_granule += 1
        assert n_granule == MIX_GRANULES and MIX_GRANULES % RING == 0
        extra = [n_slot[s] - MIX_GRANULES // RING for s in range(RING)]

        def panel_granules(i):
            name, g, tiles, granules, owner = panels[i]
            return [Granule(first_of[name, g] + j) for j in range(granules)]

        order = {(p[0], p[1]): i for i, p in enumerate(panels)}

        def wait_tile(eng, *key):
            eng.wait_ge(*ready_at[key])

        def wait_out(eng, *key):
            eng.wait_ge(*out_at[key])

        def group_tokens(row, g, t=None):
            v = row.rearrange("p (t i) -> p t i" if g == 0 else "p (i t) -> p t i", t=TT)
            return v if t is None else v[:, t]

        def in_tiles(ap):
            return ap.rearrange("p (t i) -> p t i", t=TT)

        def mixer_loads(sp):
            w_in_v = w_in.rearrange("a (k p) n -> p (a k) n", p=P)
            wba_v = w_branch_attn.rearrange("a (k p) n -> p (a k) n", p=P)
            wbs_v = w_branch_ssm.rearrange("a (k p) n -> p (a k) n", p=P)
            wo_v = w_out.rearrange("a (k p) n -> p (a k) n", p=P)
            sp.dma_start(x_t, x_rows).then_inc(xm_in, 16)
            sp.dma_start(cst[:], consts[:, 0:C_END]).then_inc(const_in, 16)
            sp.dma_start(ldrows[0:96], conv_w.rearrange("a j (f p) -> (a j f) p", p=P)).then_inc(cols_in, 16)
            sp.dma_start(ldrows[96:120], conv_b.rearrange("a (f p) -> (a f) p", p=P)).then_inc(cols_in, 16)
            sp.dma_start(ldrows2[0:8], norm_mix.rearrange("a (f p) -> (a f) p", p=P)).then_inc(cols_in, 16)
            sp.dma_start(ldrows2[8:24], gate_bias.rearrange("a (f p) -> (a f) p", p=P)).then_inc(cols_in, 16)
            sp.dma_start(ldrows2[24:40], ssm_norm_w.rearrange("a (f p) -> (a f) p", p=P)).then_inc(cols_in, 16)
            sp.dma_start(hotb, buckets).then_inc(buckets_in, 16)
            sp.wait_ge(buckets_in, 16)
            sp.dma_start(hotb[0:NBK, 3 * BR:], rel_bias).then_inc(table_rows_in, 16)
            sp.dma_start(bfull[:, 0:HID], b1[0]).then_inc(bias_raw_in, 16)
            sp.dma_start(bfull[:, HID:3072], b2[0]).then_inc(bias_raw_in, 16)

            def load_panel(i):
                name, g, tiles, granules, owner = panels[i]
                for h, gr in enumerate(panel_granules(i)):
                    if gr.reused:
                        sp.wait_ge(lo_done, gr.n - RING + 1)
                    dst = raw[:, gr.slot].rearrange("p (k n) -> p k n", k=8 if name == "bc" else 4)
                    ks = slice(4 * h, 4 * h + 4)
                    if name == "bc":
                        for part in range(2):
                            col = COL_B + 512 * part + P * g
                            sp.dma_start(dst[:, :, P * part:P * part + P], w_in_v[:, :, col:col + P])\
                                .then_inc(raw_in[gr.slot], 16)
                        continue
                    if name == "attn":
                        src = wba_v[:, 0:4, 512 * g:512 * g + 512]
                    elif name == "ssm":
                        src = wbs_v[:, 4 * (g // 2):4 * (g // 2) + 4, 512 * (g % 2):512 * (g % 2) + 512]
                    elif name == "out":
                        src = wo_v[:, ks, 512 * g:512 * g + 512]
                    else:
                        col = {"q": 0, "k": 1536, "v": 3072, "z": COL_Z, "xs": COL_X, "gate": COL_G}[name] + 512 * g
                        src = w_in_v[:, ks, col:col + 512]
                    sp.dma_start(dst, src).then_inc(raw_in[gr.slot], 16)

            def spill(g):
                for f in range(4):
                    n = 4 * g + f
                    sp.wait_ge(yt_out, n + 1)
                    sp.dma_start(yt_d[g, f], y_turn[f % 2]).then_inc(yt_saved[f % 2], 16)

            load_panel(0)
            load_panel(1)
            sp.wait_ge(ht_psum, KD)
            sp.dma_start(dtw_raw, w_in_v[:, :, COL_DT:COL_DT + NHS]).then_inc(dtw_in, 16)
            sp.wait_ge(zero_set, 1)
            sp.dma_start(tok_d.rearrange("(p n) a -> p (n a)", p=P), zero_i).then_inc(tok_zeroed, 16)
            sp.wait_ge(rel_copied, NG)
            for g in range(NG):
                sp.dma_start(bass.AP(rel_d.tensor, g * HPG * SKEW, [[SKEW, HPG], [BR + 1, P], [1, BR]]),
                             bc(rowb[:, g], [(0, P), (1, BR)])).then_inc(rel_saved, 16)
            sp.wait_ge(bias_split, 5)
            sp.dma_start(bias_d, bpart).then_inc(bias_saved, 16)
            sp.wait_ge(rel_saved, 16 * NG)
            sp.wait_ge(bias_saved, 16)
            sp.wait_ge(tok_zeroed, 16)
            for g in range(NG):
                if g:
                    sp.wait_ge(s_out, HPG * g)
                off, n = (127, 256) if g == 0 else (255, P)
                sp.dma_start(bias_t[:, :, 0:n], bass.AP(rel_d.tensor, g * HPG * SKEW + off, [[BR, P], [SKEW, HPG], [1, n]]))\
                    .then_inc(bias_in, 16)
                for i in range(3 * g + 2, 3 * g + 5):
                    load_panel(i)
            i = 3 * NG + 2
            for g in range(NSG):
                if g == 0:
                    sp.wait_ge(attn_hi, 4)
                    sp.wait_ge(attn_lo, 4)
                    for ap, src in ((dskip, d_skip), (a_neg, a_log), (dtb, dt_bias)):
                        sp.dma_start(ap, src.broadcast_to([P, NHS])).then_inc(dtc_in, 16)
                for _ in range(3):
                    if i < order["gate", 0]:
                        load_panel(i)
                        i += 1
                if g:
                    spill(g - 1)
            load_panel(order["gate", 0])
            load_panel(order["gate", 1])
            spill(NSG - 1)
            for i in range(order["gate", 2], len(panels)):
                if i == order["gate", 2]:
                    for g in range(3):
                        if g == 0:
                            sp.wait_ge(yt_saved[0], 16 * 2 * NSG)
                            sp.wait_ge(yt_saved[1], 16 * 2 * NSG)
                        sp.dma_start(y_back[g], yt_d[g].rearrange("f p s -> p f s")).then_inc(yb_in[g], 16)
                load_panel(i)
                if i == order["ssm", 1]:
                    sp.wait_ge(yb_lo, 1)
                    sp.dma_start(y_back[0], yt_d[3].rearrange("f p s -> p f s")).then_inc(yb_in[0], 16)
            sp.wait_ge(yb_lo, NSG)
            sp.dma_start(resid, x_rows).then_inc(x_in, 16)


        w1_v = w1.rearrange("a e (k p) n -> (a e) p k n", p=P)
        w2_v = w2.rearrange("a e (k p) n -> (a e) p k n", p=P)
        y_rows = y_d.rearrange("(b p) d -> b p d", p=P)
        x_rows = x.rearrange("a (t p) d -> p (a t) d", p=P)
        out_rows = out.rearrange("a (t p) d -> p (a t) d", p=P)
        h2_rows = h2_d.rearrange("(t p) d -> p t d", p=P)

        def hidden_granule(s):
            return 2 * s if s < 3 else 3 * s - 2

        class Granule:

            def __init__(self, first, passes=0, e=0):
                assert PASS_GRANULES % RING == 0 and 12 % RING == 0
                self.slot = first % RING
                self.n = first + passes * PASS_GRANULES + e * 12
                if first < MIX_GRANULES:
                    self.landed = landed_at[first]
                else:
                    turn = first // RING + passes * (PASS_GRANULES // RING) + e * (12 // RING)
                    self.landed = turn * 16 + 16 * extra[self.slot] + 16
                self.reused = first >= RING

        def split_hi(act, g):
            act.wait_ge(raw_in[g.slot], g.landed)
            if g.reused:
                act.wait_ge(granule_used, g.n - RING + 1)
            nc.scalar.activation(whi[:, g.slot], raw[:, g.slot], ACT.Copy).then_inc(hi_done, 1)

        def split_lo(dve, g):
            dve.wait_ge(hi_done, g.n + 1)
            nc.vector.tensor_tensor(wlo[:, g.slot], raw[:, g.slot], whi[:, g.slot].bitcast(F32),
                                    ALU.subtract).then_inc(lo_done, 1)

        def load(sp, g, src, shape):
            if g.reused:
                sp.wait_ge(lo_done, g.n - RING + 1)
            dst = raw[:, g.slot].rearrange("p (k n) -> p k n", k=shape)
            sp.dma_start(dst, src).then_inc(raw_in[g.slot], 16)

        def product(ps, a_hi, a_lo, b_hi, b_lo, start, stop):
            nc.tensor.matmul(ps, a_hi, b_hi, start=start, stop=False)
            nc.tensor.matmul(ps, a_hi, b_lo, start=False, stop=False)
            return nc.tensor.matmul(ps, a_lo, b_hi, start=False, stop=stop)

        def step_granules(c, passes, e, last):
            if not last:
                b0 = MIX_GRANULES + 6 + 3 * c
                return [Granule(b0, passes, e), Granule(b0 + 1, passes, e), Granule(b0 + 2, passes, e)]
            k = 4 * (NE - 1) + c
            if c == 0:
                b0 = MIX_GRANULES + 6 + 3 * k
                return [Granule(b0, passes), Granule(b0 + 1, passes), Granule(b0 + 2, passes)]
            return [Granule(MIX_GRANULES + PASS_GRANULES - 4 + c, passes)]

        def expert_loop(eng, body, passes):
            with eng.Fori(0, NE - 1) as e:
                for c in range(4):
                    body(e, c, False)
            for c in range(4):
                body(NE - 1, c, True)

        def over_passes(eng, run):
            run(0)
            eng.wait_ge(flag_ready, 1)
            more = eng.value_load(flag_i[0:1, 0:1], min_val=0, max_val=SEQ)
            with eng.If(more > CAP):
                if eng is nc.gpsimd:
                    for passes in range(1, NPASS):
                        run(passes)
                else:
                    with eng.Fori(1, NPASS) as passes:
                        run(passes)

        def first_granules(passes):
            return [Granule(MIX_GRANULES + i, passes) for i in range(6)]

        def later(passes):
            return not (isinstance(passes, int) and passes == 0)

        def conv_columns(g, j):
            return (16 + g, 20 + g, 4 * g, 4 * g + 1, 4 * g + 2, 4 * g + 3)[j]

        def conv_key(g, j):
            return ("bc", g, j) if j < 2 else ("xs", g, j - 2)

        HALO = CONV_WIDTH - 1

        def mixer_act(act):
            act.wait_ge(cols_psum, 1)
            nc.scalar.activation(cols[:, 0:120], bank[:, 6, 0:120], ACT.Copy)
            nc.scalar.activation(cols[:, 120:160], bank[:, 7, 0:40], ACT.Copy).then_inc(cols_ready, 1)
            act.wait_ge(xm_in, 16)
            for t in range(TT):
                if t == TT - 1:
                    act.wait_ge(cols_ready, 1)
                nc.scalar.activation(bank[:, 2 * t:2 * t + 2].rearrange("p a b -> p (a b)"), x_t[:, t], ACT.Square,
                                     accum_out=ms[:, t:t + 1]).then_inc(msq_done, 1)
            act.wait_ge(mrms, 1)
            nc.scalar.activation(mrstd, ms, ACT.Sqrt).then_inc(mrms, 1)

            def ahead(i):
                for gr in panel_granules(i):
                    split_hi(act, gr)

            ahead(0)
            for k in range(KD):
                act.wait_ge(ht_psum, k + 1)
                act.wait_ge(cols_ready, 1)
                nc.scalar.activation(t_hi[:, k], bank[:, k], ACT.Copy, scale=col_nm(k)).then_inc(ht_hi, 1)
            act.wait_ge(dtw_in, 16)
            nc.scalar.activation(u_hi[:, 0, 0:256], dtw_raw.rearrange("p k h -> p (k h)"), ACT.Copy).then_inc(dtw_hi, 1)
            for g in range(NG):
                act.wait_ge(rel_psum, g + 1)
                nc.scalar.activation(rowb[:, g], bank[0:HPG, 5 + g, 0:BR], ACT.Copy).then_inc(rel_copied, 1)
            act.wait_ge(dt_psum, 1)
            nc.scalar.activation(dt_raw.rearrange("p t h -> p (t h)"), bank[:, 4, 0:TT * NHS], ACT.Copy)\
                .then_inc(dt_out, 1)

            for g in range(NG):
                for name in ("q", "k", "v"):
                    i = order[name, g]
                    ahead(i + 1)
                    if name == "q" and g == 0:
                        act.wait_ge(dtw_lo, 1)
                    if name == "k" and g == 0:
                        act.wait_ge(bias_saved, 16)
                        act.wait_ge(rel_saved, 16 * NG)
                        act.wait_ge(tok_zeroed, 16)
                    for j in range(4):
                        wait_tile(act, name, g, j)
                        dst = {"q": q_t[g], "k": k_t, "v": v_t}[name][:, j]
                        scale = HEAD_DIM ** -0.5 if name == "q" else 1.0
                        nc.scalar.activation(dst, bank[:, j], ACT.Copy, scale=scale).then_inc(act_out, 1)
                if g == NG - 1:
                    ahead(order["xs", 0])
                for h in range(HPG):
                    n = HPG * g + h
                    act.wait_ge(neg_ready, n + 1)
                    if n:
                        act.wait_ge(pt_psum, n)
                    for t in range(TT):
                        src = logit_t[:, t] if g == 0 else logit_t[:, 0:2].rearrange(
                            "p a (b k) -> p (a b) k", k=P)[:, t]
                        dst = prob_t[:, t] if g == 0 else prob_t[:, 0:2].rearrange(
                            "p a (b k) -> p (a b) k", k=P)[:, t]
                        m = nc.scalar.activation(dst, src, ACT.Exp, bias=nm_t[:, t:t + 1],
                                                 accum_out=d_all[:, g, t, h:h + 1])
                    m.then_inc(p_ready, 1)
                    act.wait_ge(pt_psum, n + 1)
                    if n:
                        act.wait_ge(u_psum, n)
                    nb = 7 if g == 0 else 4
                    nc.scalar.activation(pturn[:, 0:nb].rearrange("p a b -> p (a b)"),
                                         bank[:, 6:8].rearrange("p a b -> p (a b)")[:, 0:nb * P], ACT.Copy)\
                        .then_inc(pt_out, 1)
            act.wait_ge(row_less, 1)
            nc.scalar.activation(e_row, e_row, ACT.Exp).then_inc(row_exp, 1)
            for hp in range(4):
                act.wait_ge(attn_sum, hp + 1)
                nc.scalar.activation(u_hi[:, hp], q_t[0][:, hp], ACT.Copy).then_inc(attn_hi, 1)

            act.wait_ge(sp_abs, 1)
            nc.scalar.activation(sp[1], sp[0], ACT.Exp, scale=-1.0).then_inc(sp_exp, 1)
            nc.scalar.activation(a_neg, a_neg, ACT.Exp).then_inc(sp_exp, 1)
            act.wait_ge(sp_one, 1)
            nc.scalar.activation(sp[3], sp[2], ACT.Ln).then_inc(sp_ln, 1)
            act.wait_ge(cs_psum, 1)
            nc.scalar.activation(dec3.rearrange("p a t h -> p (a t h)"), bank[:, 4, 0:3 * TT * NHS], ACT.Exp)\
                .then_inc(cs_exp, 1)

            def conv(g, j):
                n, f, key = 6 * g + j, conv_columns(g, j), conv_key(g, j)
                wait_tile(act, *key)
                if j >= 4:
                    act.wait_ge(xs_psum, 4 * g + j - 3)
                elif g and j < 2:
                    act.wait_ge(xs_psum, 4 * g - 1 + j)
                nc.scalar.activation(conv_t[n % 2], bank[:, key[2]], ACT.Identity, scale=col_cw(HALO, f),
                                     bias=col_cb(f)).then_inc(conv_on, 1)
                act.wait_ge(*out_at[key])
                dst = (b_t, c_t)[j] if j < 2 else conv_t[n % 2]
                nc.scalar.activation(dst, conv_t[n % 2], ACT.Silu).then_inc(conv_silu, 1)

            def xs_copy(g, j):
                act.wait_ge(xs_psum, 4 * g + j + 1)
                nc.scalar.activation(xs[:, :, P * j:P * j + P],
                                     bank[:, 4 + j % 2].rearrange("p (c f) -> p c f", c=TT), ACT.Copy).then_inc(xs_out, 1)

            def turned(g):
                for f in range(4):
                    n = 4 * g + f
                    act.wait_ge(yt_psum, n + 1)
                    if n >= 2:
                        act.wait_ge(yt_saved[f % 2], 16 * (n // 2))
                    nc.scalar.activation(y_turn[f % 2], bank[:, 6 + f % 2], ACT.Copy, scale=col_sn(4 * g + f))\
                        .then_inc(yt_out, 1)

            for g in range(NSG):
                conv(g, 0)
                conv(g, 1)
                ahead(order["z", g])
                for j in range(4):
                    conv(g, 2 + j)
                    if j:
                        xs_copy(g, j - 1)
                if g:
                    turned(g - 1)
                xs_copy(g, 3)
                act.wait_ge(bt_psum, g + 1)
                nc.scalar.activation(b_tok.rearrange("p c n -> p (c n)"), bank[:, 7], ACT.Copy).then_inc(bt_out, 1)
                for t in range(TT):
                    wait_tile(act, "z", g, t)
                    nc.scalar.activation(zs[:, t], bank[:, t], ACT.Silu).then_inc(act_out, 1)
                ahead(order["z", g] + 1)
                if g < NSG - 1:
                    ahead(order["z", g] + 2)
                for c in range(TT):
                    i = TT * g + c
                    act.wait_ge(seg_psum, i + 1)
                    if i >= 2:
                        act.wait_ge(diag_psum, i - 1)
                    nc.scalar.activation(dec[i % 2].rearrange("p h l -> p (h l)"),
                                         bank[:, 4:6].rearrange("p a b -> p (a b)"), ACT.Exp).then_inc(dec_ready, 1)
                for c in range(TT):
                    act.wait_ge(y_chunk, TT * g + c + 1)
                    nc.scalar.activation(xs[:, c], zs[:, c], ACT.Square, accum_out=gss[:, c:c + 1]).then_inc(gsq_done, 1)
                act.wait_ge(grms, 2 * g + 1)
                nc.scalar.activation(grstd, gss, ACT.Sqrt).then_inc(grms, 1)

            for i in range(4):
                if i < 3:
                    ahead(order["gate", i + 1])
                else:
                    ahead(order["attn", 0])
                    ahead(order["attn", 1])
                if i == 0:
                    turned(NSG - 1)
                for j in range(4):
                    f = 4 * i + j
                    wait_tile(act, "gate", i, j)
                    nc.scalar.activation(gates[:, f // KD, f % KD], bank[:, j], ACT.Sigmoid, bias=col_gb(f))\
                        .then_inc(act_out, 1)
            ahead(order["ssm", 0])
            ahead(order["ssm", 1])

            def rows_back(g, dst, until):
                act.wait_ge(yb_in[g % 3], 16 * (g // 3 + 1))
                act.wait_ge(granule_used, until)
                nc.scalar.activation(dst, y_back[g % 3], ACT.Copy).then_inc(yb_hi, 1)

            rows_back(0, t_hi[:, 0:4], first_of["attn", 0])
            rows_back(1, t_hi[:, 4:8], first_of["attn", 0])
            ahead(order["ssm", 2])
            ahead(order["ssm", 3])
            rows_back(2, u_hi[:], first_of["ssm", 0])
            ahead(order["ssm", 4])
            ahead(order["ssm", 5])
            rows_back(3, t_hi[:, 0:4], first_of["ssm", 2])
            ahead(order["ssm", 6])
            ahead(order["ssm", 7])
            ahead(order["out", 0])
            ahead(order["out", 1])
            act.wait_ge(granule_used, first_of["out", 0])
            for f in range(KD):
                act.wait_ge(merged_f, f + 1)
                nc.scalar.activation(t_hi[:, f], gates[:, 1, f], ACT.Copy).then_inc(merged_hi, 1)

        def mixer_pool(pool):
            nc.gpsimd.memset(zero_i, 0).then_inc(zero_set, 1)
            for g in range(NSG):
                hs = slice(HPG * g, HPG * g + HPG)
                for c in range(TT):
                    i = TT * g + c
                    if c == 0 and g == 0:
                        pool.wait_ge(a_ready, 1)
                        pool.wait_ge(cs_exp, 1)
                        pool.wait_ge(dtc_in, 48)
                    if i:
                        pool.wait_ge(seg_psum, i)
                    nc.gpsimd.tensor_tensor(ramp, bc(tri_le, [(0, HPG), (1, P)]),
                                            bc(a_d[:, c, hs], [(1, HPG), (0, P)]), ALU.mult).then_inc(ramp_ready, 1)
                    if c == 0:
                        pool.wait_ge(xs_out, 4 * g + 4)
                    if i >= 2:
                        pool.wait_ge(diag_psum, i - 1)
                    x3 = xs[:, c].rearrange("p (h q) -> p h q", h=HPG)
                    xd3 = xd[i % 2].rearrange("p (h q) -> p h q", h=HPG)
                    nc.gpsimd.tensor_tensor(xd3, x3, bc(dts[:, c, hs], [(1, HPG), (0, 64)]), ALU.mult)\
                        .then_inc(xd_ready, 1)
                    if c < TT - 1:
                        pool.wait_ge(xd_ready, i + 1)
                        if 3 * g + c:
                            pool.wait_ge(st_psum, 3 * g + c)
                        nc.gpsimd.tensor_tensor(xdd.rearrange("p (h q) -> p h q", h=HPG), xd3,
                                                bc(dec3[:, 1, c, hs], [(1, HPG), (0, 64)]), ALU.mult)\
                            .then_inc(xdd_ready, 1)
                    if i:
                        pool.wait_ge(skip_used, i)
                    nc.gpsimd.tensor_tensor(skip.rearrange("p (h q) -> p h q", h=HPG), x3,
                                            bc(dskip[:, hs], [(1, HPG), (0, 64)]), ALU.mult).then_inc(skip_ready, 1)

        def mixer_dve(dve, link):
            dve.wait_ge(msq_done, TT)
            nc.vector.tensor_scalar(ms, ms, 1.0 / D, EPS, ALU.mult, ALU.add).then_inc(mrms, 1)
            dve.wait_ge(mrms, 2)
            link(nc.vector.reciprocal(mrstd, mrstd))
            for t in range(TT):
                nc.vector.tensor_scalar(x_t[:, t], x_t[:, t], mrstd[:, t:t + 1], None, ALU.mult).then_inc(xn_ready, 1)

            def ahead(i):
                for gr in panel_granules(i):
                    split_lo(dve, gr)

            dve.wait_ge(bias_raw_in, 32)
            for q in range(2):
                link(nc.vector.tensor_copy(bpart[:, q], bfull))
                link(nc.vector.tensor_tensor(bfull, bfull, bpart[:, q], ALU.subtract))
            nc.vector.tensor_copy(bpart[:, 2], bfull).then_inc(bias_split, 5)
            ahead(0)
            for k in range(KD):
                dve.wait_ge(ht_hi, k + 1)
                nc.vector.scalar_tensor_tensor(out=t_lo[:, k], in0=bank[:, k], scalar=col_nm(k),
                                               in1=t_hi[:, k].bitcast(F32), op0=ALU.mult, op1=ALU.subtract)\
                    .then_inc(ht_lo, 1)
            dve.wait_ge(dtw_hi, 1)
            nc.vector.tensor_tensor(u_lo[:, 0, 0:256], dtw_raw.rearrange("p k h -> p (k h)"),
                                    u_hi[:, 0, 0:256].bitcast(F32), ALU.subtract).then_inc(dtw_lo, 1)

            def outputs_back(g, hp):
                dve.wait_ge(u_psum, HPG * g + 2 * hp + 2)
                nc.vector.tensor_copy(group_tokens(q_t[g][:, hp], g), in_tiles(bank[:, hp % 2])).then_inc(u_out, 1)

            for g in range(NG):
                for name in ("q", "k", "v"):
                    ahead(order[name, g] + 1)
                if g == 0:
                    dve.wait_ge(bias_in, 16)
                    nc.vector.memset(logit_t[:, 0, 0:P], -BIG)
                if g == NG - 1:
                    ahead(order["xs", 0])
                for h in range(HPG):
                    n = HPG * g + h
                    b0 = 4 if h % 2 == 0 else 2
                    dve.wait_ge(s_psum, n + 1)
                    dve.wait_ge(bias_in, 16 * (g + 1))
                    if n:
                        dve.wait_ge(p_ready, n)
                    if g == 0:
                        s4 = bank[:, b0:b0 + 2].rearrange("p a (t k) -> p (a t) k", t=2)
                        nc.vector.tensor_tensor(logit_t[:, 0, P:], s4[:, 0, P:], bias_t[:, h, P:], ALU.add)
                        nc.vector.tensor_tensor(logit_t[:, 1:4], s4[:, 1:4], bc(bias_t[:, h], [(0, 3), (1, 2 * P)]),
                                                ALU.add).then_inc(s_out, 1)
                        lg = logit_t
                    else:
                        lg = logit_t[:, 0:2].rearrange("p a (b k) -> p (a b) k", k=P)
                        nc.vector.tensor_tensor(lg, bank[:, b0].rearrange("p (t k) -> p t k", t=TT),
                                                bc(bias_t[:, h, 0:P], [(0, TT), (1, P)]), ALU.add).then_inc(s_out, 1)
                    dve.wait_ge(s_out, n + 1)
                    link(nc.vector.tensor_reduce(m_all[:, g, :, h], lg, AX.X, ALU.max))
                    nc.vector.tensor_scalar(nm_t, m_all[:, g, :, h], -1.0, None, ALU.mult).then_inc(neg_ready, 1)
                    if h >= 3 and h % 2:
                        outputs_back(g, (h - 3) // 2)
                outputs_back(g, 3)

            for g in range(NG):
                for kind, row in ((0, m_row), (1, d_row)):
                    dve.wait_ge(row_psum, 2 * g + kind + 1)
                    nc.vector.tensor_copy(group_tokens(row[:, g], g), in_tiles(bank[0:HPG, 3 * kind + g]))\
                        .then_inc(row_out, 1)
            dve.wait_ge(row_out, 2 * NG)
            link(nc.vector.tensor_tensor(top_row, m_row[:, 0], m_row[:, 1], ALU.max))
            link(nc.vector.tensor_tensor(top_row, top_row, m_row[:, 2], ALU.max))
            nc.vector.tensor_tensor(e_row, m_row, bc(top_row, [(0, NG), (1, SEQ)]), ALU.subtract).then_inc(row_less, 1)
            dve.wait_ge(row_exp, 1)
            link(nc.vector.tensor_tensor(d_row, d_row, e_row, ALU.mult))
            link(nc.vector.tensor_tensor(z_row, d_row[:, 0], d_row[:, 1], ALU.add))
            link(nc.vector.tensor_tensor(z_row, z_row, d_row[:, 2], ALU.add))
            link(nc.vector.reciprocal(z_row, z_row))
            nc.vector.tensor_tensor(e_row, e_row, bc(z_row, [(0, NG), (1, SEQ)]), ALU.mult).then_inc(share_ready, 1)
            for hp in range(4):
                for g in range(NG):
                    n = NG * hp + g
                    dve.wait_ge(share_psum, n + 1)
                    nc.vector.tensor_tensor(q_t[g][:, hp], q_t[g][:, hp], bank[:, n % 8], ALU.mult)\
                        .then_inc(share_used, 1)
                dve.wait_ge(share_used, NG * hp + NG)
                link(nc.vector.tensor_tensor(q_t[0][:, hp], q_t[0][:, hp], q_t[1][:, hp], ALU.add))
                nc.vector.tensor_tensor(q_t[0][:, hp], q_t[0][:, hp], q_t[2][:, hp], ALU.add).then_inc(attn_sum, 1)
                dve.wait_ge(attn_hi, hp + 1)
                nc.vector.tensor_tensor(u_lo[:, hp], q_t[0][:, hp], u_hi[:, hp].bitcast(F32), ALU.subtract)\
                    .then_inc(attn_lo, 1)

            dve.wait_ge(dtc_in, 48)
            dve.wait_ge(dt_out, 1)
            link(nc.vector.tensor_tensor(dts, dt_raw, bc(dtb, [(0, TT), (1, NHS)]), ALU.add))
            nc.vector.scalar_tensor_tensor(out=sp[0], in0=dts, scalar=-1.0, in1=dts, op0=ALU.mult, op1=ALU.max)\
                .then_inc(sp_abs, 1)
            dve.wait_ge(sp_exp, 1)
            nc.vector.tensor_scalar(sp[2], sp[1], 1.0, None, ALU.add).then_inc(sp_one, 1)
            dve.wait_ge(sp_one, 1)
            link(nc.vector.scalar_tensor_tensor(out=sp[0], in0=sp[2], scalar=-1.0, in1=sp[1], op0=ALU.add,
                                                op1=ALU.subtract))
            dve.wait_ge(sp_ln, 1)
            link(nc.vector.tensor_tensor(sp[3], sp[3], sp[0], ALU.subtract))
            link(nc.vector.scalar_tensor_tensor(out=dts, in0=dts, scalar=0.0, in1=sp[3], op0=ALU.max, op1=ALU.add))
            dve.wait_ge(sp_exp, 2)
            nc.vector.scalar_tensor_tensor(out=a_d, in0=dts, scalar=-1.0, in1=bc(a_neg, [(0, TT), (1, NHS)]),
                                           op0=ALU.mult, op1=ALU.mult).then_inc(a_ready, 1)

            def conv(g, j):
                n, f, key = 6 * g + j, conv_columns(g, j), conv_key(g, j)
                dve.wait_ge(conv_on, n + 1)
                for back in range(1, CONV_WIDTH):
                    m = nc.vector.scalar_tensor_tensor(
                        out=conv_t[n % 2][:, back:], in0=bank[:, key[2], 0:SEQ - back], scalar=col_cw(HALO - back, f),
                        in1=conv_t[n % 2][:, back:], op0=ALU.mult, op1=ALU.add)
                    if back < HALO:
                        link(m)
                m.then_inc(dve_out, 1)

            def heads(ap):
                return ap.rearrange("p (h q) -> p h q", h=HPG)

            for g in range(NSG):
                hs = slice(HPG * g, HPG * g + HPG)
                conv(g, 0)
                conv(g, 1)
                ahead(order["z", g])
                for j in range(4):
                    conv(g, 2 + j)
                dve.wait_ge(cb_psum, g + 1)
                nc.vector.tensor_tensor(cbm, bank[:, 6].rearrange("p (c l) -> p c l", c=TT),
                                        bc(tri_le, [(0, TT), (1, P)]), ALU.mult).then_inc(cb_out, 1)
                ahead(order["z", g] + 1)
                if g < NSG - 1:
                    ahead(order["z", g] + 2)
                dve.wait_ge(cb_out, g + 1)
                dve.wait_ge(cs_exp, 1)
                for c in range(TT):
                    i = TT * g + c
                    dve.wait_ge(dec_ready, i + 1)
                    nc.vector.tensor_tensor(dec[i % 2], dec[i % 2], bc(cbm[:, c], [(0, HPG), (1, P)]), ALU.mult)\
                        .then_inc(mat_ready, 1)
                    if c:
                        dve.wait_ge(off_psum, 3 * g + c)
                        dve.wait_ge(y_chunk, i)
                        nc.vector.tensor_tensor(heads(y_t), heads(bank[:, 2]), bc(dec3[:, 0, c, hs], [(1, HPG), (0, 64)]),
                                                ALU.mult).then_inc(off_used, 1)
                    if c < TT - 1:
                        if c:
                            link(nc.vector.tensor_tensor(heads(state), heads(state),
                                                         bc(dec3[:, 2, c, hs], [(1, HPG), (0, 64)]), ALU.mult))
                        dve.wait_ge(st_psum, 3 * g + c + 1)
                        if c:
                            nc.vector.tensor_tensor(state, state, bank[:, 3], ALU.add).then_inc(st_used, 1)
                        else:
                            nc.vector.tensor_copy(state, bank[:, 3]).then_inc(st_used, 1)
                    dve.wait_ge(skip_ready, i + 1)
                    if c:
                        dve.wait_ge(off_used, 3 * g + c)
                        nc.vector.tensor_tensor(y_t, y_t, skip, ALU.add).then_inc(skip_used, 1)
                        dve.wait_ge(skip_used, i + 1)
                        dve.wait_ge(diag_psum, i + 1)
                        link(nc.vector.tensor_tensor(y_t, y_t, bank[:, i % 2], ALU.add))
                    else:
                        if g:
                            dve.wait_ge(y_chunk, i)
                        dve.wait_ge(diag_psum, i + 1)
                        nc.vector.tensor_tensor(y_t, bank[:, i % 2], skip, ALU.add).then_inc(skip_used, 1)
                        dve.wait_ge(skip_used, i + 1)
                    wait_out(dve, "z", g, c)
                    nc.vector.tensor_tensor(zs[:, c], y_t, zs[:, c], ALU.mult).then_inc(y_chunk, 1)
                dve.wait_ge(gsq_done, TT * g + TT)
                nc.vector.tensor_scalar(gss, gss, 1.0 / 512, EPS, ALU.mult, ALU.add).then_inc(grms, 1)
                dve.wait_ge(grms, 2 * g + 2)
                link(nc.vector.reciprocal(grstd, grstd))
                for c in range(TT):
                    nc.vector.tensor_scalar(zs[:, c], zs[:, c], grstd[:, c:c + 1], None, ALU.mult).then_inc(yn_ready, 1)

            for i in range(3):
                ahead(order["gate", i + 1])
            ahead(order["attn", 0])
            ahead(order["attn", 1])
            ahead(order["ssm", 0])
            ahead(order["ssm", 1])

            def rows_back(g, hi, lo):
                dve.wait_ge(yb_hi, g + 1)
                nc.vector.tensor_tensor(lo, y_back[g % 3], hi.bitcast(F32), ALU.subtract).then_inc(yb_lo, 1)

            rows_back(0, t_hi[:, 0:4], t_lo[:, 0:4])
            rows_back(1, t_hi[:, 4:8], t_lo[:, 4:8])
            for f in range(KD):
                wait_tile(dve, "attn", f // 4, f % 4)
                wait_out(dve, "gate", f // 4, f % 4)
                nc.vector.tensor_tensor(gates[:, 0, f], gates[:, 0, f], bank[:, f], ALU.mult).then_inc(dve_out, 1)
            ahead(order["ssm", 2])
            ahead(order["ssm", 3])
            rows_back(2, u_hi[:], u_lo[:])
            ahead(order["ssm", 4])
            ahead(order["ssm", 5])
            rows_back(3, t_hi[:, 0:4], t_lo[:, 0:4])
            ahead(order["ssm", 6])
            ahead(order["ssm", 7])
            ahead(order["out", 0])
            for f in range(KD):
                wait_tile(dve, "ssm", 6 + f // 4, f % 4)
                wait_out(dve, "gate", 2 + f // 4, f % 4)
                nc.vector.tensor_tensor(gates[:, 1, f], gates[:, 1, f], bank[:, f], ALU.mult).then_inc(dve_out, 1)
                wait_out(dve, "ssm", 6 + f // 4, f % 4)
                nc.vector.tensor_tensor(gates[:, 1, f], gates[:, 1, f], gates[:, 0, f], ALU.add).then_inc(merged_f, 1)
            for f in range(KD):
                dve.wait_ge(merged_hi, f + 1)
                nc.vector.tensor_tensor(t_lo[:, f], gates[:, 1, f], t_hi[:, f].bitcast(F32), ALU.subtract)\
                    .then_inc(merged_lo, 1)
            ahead(order["out", 1])
            dve.wait_ge(x_in, 16)
            for h in range(2):
                for t in range(TT):
                    wait_tile(dve, "out", h, t)
                    nc.vector.tensor_tensor(resid[:, t, 512 * h:512 * h + 512], resid[:, t, 512 * h:512 * h + 512],
                                            bank[:, 4 * h + t], ALU.add).then_inc(dve_out, 1)

        def mixer_pe(pe):
            pe.wait_ge(const_in, 16)
            pe.wait_ge(cols_in, 80)
            nc.tensor.transpose(bank[:, 6, 0:120], ldrows[0:120], ident[0:120, 0:120])
            nc.tensor.transpose(bank[:, 7, 0:40], ldrows2[0:40], ident[0:40, 0:40]).then_inc(cols_psum, 1)
            pe.wait_ge(cols_ready, 1)
            for t in range(TT):
                pe.wait_ge(xn_ready, t + 1)
                for k in range(KD):
                    m = nc.tensor.transpose(bank[:, k, t * P:(t + 1) * P], x_t[:, t, k * P:(k + 1) * P], ident)
                    if t == TT - 1:
                        m.then_inc(ht_psum, 1)
            pe.wait_ge(ht_lo, KD)
            pe.wait_ge(table_rows_in, 16)
            for g in range(NG):
                nc.tensor.matmul(bank[0:HPG, 5 + g, 0:BR], hotb[:, 3 * BR + HPG * g:3 * BR + HPG * g + HPG],
                                 hotb[:, BR * g:BR * g + BR], start=True, stop=True).then_inc(rel_psum, 1)
            pe.wait_ge(dtw_lo, 1)
            for t in range(TT):
                for k in range(KD):
                    m = product(bank[:, 4, t * NHS:(t + 1) * NHS], t_hi[:, k, t * P:(t + 1) * P],
                                t_lo[:, k, t * P:(t + 1) * P], u_hi[:, 0, k * NHS:(k + 1) * NHS],
                                u_lo[:, 0, k * NHS:(k + 1) * NHS], k == 0, k == KD - 1)
            m.then_inc(dt_psum, 1)

            def panel(name, g, one_tile, before=None, after=None, banks=0):
                i = order[name, g]
                _, _, tiles, granules, _ = panels[i]
                gr = panel_granules(i)
                steps = 4 if name in ("attn", "ssm") else KD
                per = steps // granules
                for j in range(tiles):
                    if before:
                        before(j)
                    for k in range(steps):
                        w = gr[k // per]
                        if j == 0 and k % per == 0:
                            pe.wait_ge(lo_done, w.n + 1)
                        start, stop = k == 0, k == steps - 1
                        if name == "ssm":
                            start, stop = start and g < 2, stop and g >= 6
                        m = product(bank[:, banks + j], *one_tile(j, k, w, k % per), start, stop)
                        if j == tiles - 1 and k % per == per - 1:
                            m.then_inc(granule_used, 1)
                    if j < tiles - 1:
                        m.then_inc(tile_done, 1)
                    if after:
                        after(j)

            def channels(act_hi, act_lo, width=512):
                def operands(j, k, w, kk):
                    cols_w = slice(width * kk + P * j, width * kk + P * j + P)
                    return whi[:, w.slot, cols_w], wlo[:, w.slot, cols_w], act_hi(k), act_lo(k)
                return operands

            def tokens(act_hi, act_lo):
                def operands(t, k, w, kk):
                    cols_w = slice(512 * kk, 512 * kk + 512)
                    return act_hi(t, k), act_lo(t, k), whi[:, w.slot, cols_w], wlo[:, w.slot, cols_w]
                return operands

            from_h = channels(lambda k: t_hi[:, k], lambda k: t_lo[:, k])

            for g in range(NG):
                def q_banks(j):
                    if g and j == 0:
                        pe.wait_ge(u_out, 4 * g)
                        pe.wait_ge(s_out, HPG * g)

                panel("q", g, from_h, q_banks)
                panel("k", g, from_h, lambda j: wait_out(pe, "q", g, j))
                panel("v", g, tokens(lambda t, k: group_tokens(t_hi[:, k], g, t),
                                     lambda t, k: group_tokens(t_lo[:, k], g, t)),
                      lambda j: wait_out(pe, "k", g, j))

                def scores(h):
                    n, hp, rows = HPG * g + h, h // 2, slice(64 * (h % 2), 64 * (h % 2) + 64)
                    b0 = 4 if h % 2 == 0 else 2
                    if h == 0:
                        wait_out(pe, "v", g, 3)
                        pe.wait_ge(dt_out, 1)
                        if g == 0:
                            pe.wait_ge(rel_copied, NG)
                    if n >= 2:
                        pe.wait_ge(s_out, n - 1)
                    for t in range(TT):
                        q1 = group_tokens(q_t[g][rows, hp], g, t)
                        if g == 0:
                            lo_k, lo_c = (t - 1) * P, 256 * (t % 2)
                            if t == 0:
                                lo_k, lo_c = 0, P
                            hi_k = (t + 1) * P
                            m = nc.tensor.matmul(bank[:, b0 + t // 2, lo_c:lo_c + hi_k - lo_k], q1,
                                                 k_t[rows, hp, lo_k:hi_k], start=True, stop=True)
                        else:
                            m = nc.tensor.matmul(bank[:, b0, P * t:P * t + P], q1, group_tokens(k_t[rows, hp], g, t),
                                                 start=True, stop=True)
                    m.then_inc(s_psum, 1)

                if g == 0:
                    blocks = [(0, 0, P)] + [(t, t - 1 + a, P * a) for t in range(1, TT) for a in range(2)]
                else:
                    blocks = [(t, t, 0) for t in range(TT)]

                def turn_probs(h):
                    n = HPG * g + h
                    pe.wait_ge(p_ready, n + 1)
                    if n:
                        pe.wait_ge(pt_out, n)
                    pr = prob_t if g == 0 else prob_t[:, 0:2].rearrange("p a (b k) -> p (a b) k", k=P)
                    for b, (t, kt, c0) in enumerate(blocks):
                        m = nc.tensor.transpose(bank[:, 6 + b // 4, P * (b % 4):P * (b % 4) + P],
                                                pr[:, t, c0:c0 + P], ident)
                    m.then_inc(pt_psum, 1)

                def values(h):
                    n, hp, r0 = HPG * g + h, h // 2, 64 * (h % 2)
                    if h >= 4 and h % 2 == 0:
                        pe.wait_ge(u_out, 4 * g + hp - 1)
                    pe.wait_ge(pt_out, n + 1)
                    for b, (t, kt, c0) in enumerate(blocks):
                        first = b == 0 or blocks[b - 1][0] != t
                        last = b == len(blocks) - 1 or blocks[b + 1][0] != t
                        m = nc.tensor.matmul(bank[r0:r0 + 64, hp % 2, P * t:P * t + P], v_t[:, kt, 64 * h:64 * h + 64],
                                             pturn[:, b], start=first, stop=last)
                    m.then_inc(u_psum, 1)

                scores(0)
                for h in range(HPG):
                    if h < HPG - 1:
                        scores(h + 1)
                    turn_probs(h)
                    if h:
                        values(h - 1)
                values(HPG - 1)

            pe.wait_ge(u_out, 4 * NG)
            pe.wait_ge(s_out, HPG * NG)
            for g in range(NG):
                for kind, src in ((0, m_all), (1, d_all)):
                    for t in range(TT):
                        m = nc.tensor.transpose(bank[0:HPG, 3 * kind + g, P * t:P * t + P], src[:, g, t], ident)
                    m.then_inc(row_psum, 1)
            pe.wait_ge(share_ready, 1)
            for hp in range(4):
                for g in range(NG):
                    n = NG * hp + g
                    if n >= 8:
                        pe.wait_ge(share_used, n - 7)
                    for half in range(2):
                        m = nc.tensor.matmul(bank[64 * half:64 * half + 64, n % 8],
                                             bc(ident[0:HPG, 2 * hp + half:2 * hp + half + 1], [(0, 64)]),
                                             e_row[:, g], start=True, stop=True)
                    m.then_inc(share_psum, 1)
            pe.wait_ge(share_used, 4 * NG)

            def turned(g):
                for f in range(4):
                    n = 4 * g + f
                    if f == 0:
                        pe.wait_ge(yn_ready, TT * g + TT)
                    if n >= 2:
                        pe.wait_ge(yt_out, n - 1)
                    for c in range(TT):
                        m = nc.tensor.transpose(bank[:, 6 + f % 2, P * c:P * c + P], zs[:, c, P * f:P * f + P], ident)
                    m.then_inc(yt_psum, 1)

            for g in range(NSG):
                def x_turn(j):
                    n = 4 * g + j
                    if j < 2 and g:
                        pe.wait_ge(dec_ready, TT * g)
                    if j < 2 and g == 0:
                        pe.wait_ge(cs_exp, 1)
                    if j >= 2:
                        pe.wait_ge(xs_out, n - 1)
                    pe.wait_ge(conv_silu, 6 * g + 3 + j)
                    for c in range(TT):
                        m = nc.tensor.transpose(bank[:, 4 + j % 2, P * c:P * c + P],
                                                conv_t[j % 2][:, P * c:P * c + P], ident)
                    m.then_inc(xs_psum, 1)

                def bc_banks(j):
                    if g:
                        pe.wait_ge(y_chunk, TT * g)

                panel("bc", g, channels(lambda k: t_hi[:, k], lambda k: t_lo[:, k], 256), bc_banks)
                if g == 0:
                    pe.wait_ge(a_ready, 1)
                    flat = a_d.rearrange("p t h -> p (t h)")
                    for q, lhs in enumerate((tri_le, tri_gt, ones)):
                        m = nc.tensor.matmul(bank[:, 4, P * q:P * q + P], lhs, flat, start=True, stop=True)
                    m.then_inc(cs_psum, 1)

                def xs_banks(j):
                    if j < 2:
                        wait_out(pe, "bc", g, j)

                panel("xs", g, from_h, xs_banks, lambda j: x_turn(j - 1) if j else None)
                if g:
                    turned(g - 1)
                x_turn(3)
                if g:
                    pe.wait_ge(yt_out, 4 * g)
                for c in range(TT):
                    m = nc.tensor.transpose(bank[:, 7, P * c:P * c + P], b_t[:, P * c:P * c + P], ident)
                m.then_inc(bt_psum, 1)
                for c in range(TT):
                    m = nc.tensor.matmul(bank[:, 6, P * c:P * c + P], b_t[:, P * c:P * c + P], c_t[:, P * c:P * c + P],
                                         start=True, stop=True)
                m.then_inc(cb_psum, 1)
                panel("z", g, tokens(lambda t, k: t_hi[:, k, P * t:P * t + P], lambda t, k: t_lo[:, k, P * t:P * t + P]),
                      lambda j: wait_out(pe, "xs", g, j))
                wait_out(pe, "z", g, 3)

                def segments(c):
                    i = TT * g + c
                    pe.wait_ge(ramp_ready, i + 1)
                    if c == 0:
                        pe.wait_ge(xs_out, 4 * g + 4)
                    if i:
                        pe.wait_ge(dec_ready, i)
                    for a in range(2):
                        m = nc.tensor.matmul(bank[:, 4 + a], tri_gt,
                                             ramp[:, 4 * a:4 * a + 4].rearrange("p h l -> p (h l)"), start=True, stop=True)
                    m.then_inc(seg_psum, 1)

                segments(0)
                for c in range(TT):
                    i = TT * g + c
                    if c < TT - 1:
                        segments(c + 1)
                    if c:
                        pe.wait_ge(st_used, 3 * g + c)
                        if c > 1:
                            pe.wait_ge(off_used, 3 * g + c - 1)
                        nc.tensor.matmul(bank[:, 2], c_t[:, P * c:P * c + P], state, start=True, stop=True)\
                            .then_inc(off_psum, 1)
                    if c < TT - 1:
                        pe.wait_ge(xdd_ready, 3 * g + c + 1)
                        pe.wait_ge(bt_out, g + 1)
                        nc.tensor.matmul(bank[:, 3], b_tok[:, c], xdd, start=True, stop=True).then_inc(st_psum, 1)
                    pe.wait_ge(mat_ready, i + 1)
                    pe.wait_ge(xd_ready, i + 1)
                    if c >= 2:
                        pe.wait_ge(y_chunk, i - 1)
                    for h in range(HPG):
                        m = nc.tensor.matmul(bank[:, i % 2, 64 * h:64 * h + 64], dec[i % 2][:, h],
                                             xd[i % 2][:, 64 * h:64 * h + 64], start=True, stop=True)
                    m.then_inc(diag_psum, 1)

            for i in range(4):
                panel("gate", i, from_h,
                      (lambda j: wait_out(pe, "gate", i - 1, j)) if i else (lambda j: pe.wait_ge(y_chunk, TT * NSG)))
                if i == 0:
                    turned(NSG - 1)
            for h in range(2):
                def attn_banks(j):
                    if h == 0:
                        wait_out(pe, "gate", 3, j)
                    elif j == 0:
                        pe.wait_ge(yt_out, 4 * NSG)
                panel("attn", h, channels(lambda k: u_hi[:, k], lambda k: u_lo[:, k]), attn_banks, banks=4 * h)
            for g in range(NSG):
                pe.wait_ge(yb_lo, g + 1)
                hi, lo, k0 = ((t_hi, t_lo, 0), (t_hi, t_lo, 4), (u_hi, u_lo, 0), (t_hi, t_lo, 0))[g]
                for h in range(2):
                    panel("ssm", 2 * g + h, channels(lambda k: hi[:, k0 + k], lambda k: lo[:, k0 + k]),
                          (lambda j: wait_out(pe, "attn", h, j)) if g == 0 else None, banks=4 * h)
            pe.wait_ge(merged_lo, KD)
            for h in range(2):
                panel("out", h, tokens(lambda t, k: t_hi[:, k, P * t:P * t + P], lambda t, k: t_lo[:, k, P * t:P * t + P]),
                      lambda j: wait_out(pe, "ssm", 6 + h, j), banks=4 * h)

        block = ctx.enter_context(nc.Block())

        @block.sync
        def _(sp):
            mixer_loads(sp)
            sp.wait_ge(merged_lo, KD)
            sp.dma_start(wffn, norm_ffn.broadcast_to([P, D])).then_inc(norm_in, 16)
            sp.dma_start(rw, router_w.rearrange("a (k p) e -> p (a k) e", p=P)).then_inc(router_in, 16)
            sp.dma_start(rb, router_b.broadcast_to([P, NE])).then_inc(router_in, 16)
            sp.dma_start(late, consts[:, C_END:C_ALL]).then_inc(late_in, 16)

            def hidden(g, e, c, half):
                load(sp, g, w1_v[e, :, 4 * half:4 * half + 4, 512 * c:512 * c + 512], 4)

            def run(passes):
                if later(passes):
                    sp.wait_ge(comb_used, passes * TT * TOPK)
                g = first_granules(passes)
                for s in range(3):
                    hidden(g[2 * s], 0, s, 0)
                    hidden(g[2 * s + 1], 0, s, 1)

                def body(e, c, last):
                    g = step_granules(c, passes, e, last)
                    load(sp, g[0], w2_v[e, :, 2 * c:2 * c + 2, :], 2)
                    if len(g) == 3:
                        ahead = e if c == 0 else e + 1
                        hidden(g[1], ahead, (c + 3) % 4, 0)
                        hidden(g[2], ahead, (c + 3) % 4, 1)

                if not later(passes):
                    pass
                expert_loop(sp, body, passes)

            over_passes(sp, run)
            sp.wait_ge(h2_ready, TT)
            sp.dma_start(wfin, norm_final.unsqueeze(0).broadcast_to([P, D])).then_inc(fin_in, 16)
            sp.wait_ge(out_ready, TT)
            sp.dma_start(out_rows, resid).then_inc(out_saved, 16)
            sp.wait_ge(out_saved, 16)

        @block.gpsimd
        def _(pool):
            mixer_pool(pool)
            pool.wait_ge(h2_ready, TT)
            nc.gpsimd.iota(tokc, [[P, TT]], base=0, channel_multiplier=1).then_inc(ids_set, 1)
            pool.wait_ge(ids_set, 1)
            pool.wait_ge(tok_zeroed, 16)
            pool.wait_ge(places_ready, 1)
            for j in range(TT * TOPK):
                pool.indirect_dma_start(tok_d, bass.IndirectOffsetOnAxis(place_i[:, j:j + 1], 0),
                                        tokc[:, j // TOPK:j // TOPK + 1], None).then_inc(tok_saved, 16)
            pool.wait_ge(tok_saved, 16 * TT * TOPK)
            pool.dma_start(table, tok_d.rearrange("(b p e) a -> p b (e a)", b=NPASS, p=P)).then_inc(table_in, 16)
            pool.wait_ge(table_in, 16)
            pool.wait_ge(h2_saved, 16)
            pool.wait_ge(bias_saved, 16)

            def gather(passes, e, first):
                n = passes * NE + e
                if not first:
                    pool.wait_ge(xg_in, n * 16)
                    pool.wait_ge(xt_psum, n)
                nc.gpsimd.tensor_copy(idx, table[:, passes, bass.ds(e, 1)])
                pool.drain()
                pool.indirect_dma_start(xg.rearrange("p k s -> p (k s)"), None, h2_d,
                                        bass.IndirectOffsetOnAxis(idx, 0)).then_inc(xg_in, 16)

            def run(passes):
                gather(passes, 0, not later(passes))
                with pool.Fori(1, NE) as e:
                    gather(passes, e, False)
                pool.wait_ge(y_saved, (passes * NE + NE + 1) * 16)
                for j in range(TT * TOPK):
                    if j >= 8:
                        pool.wait_ge(comb_used, passes * TT * TOPK + j - 7)
                    pool.indirect_dma_start(raw[:, (j % 8) // 2, 1024 * (j % 2):1024 * (j % 2) + 1024], None, y_d,
                                            bass.IndirectOffsetOnAxis(slot_i[:, j:j + 1], 0))\
                        .then_inc(comb_in[j % 8], 16)

            over_passes(pool, run)
        @block.scalar
        def _(act):
            act.sem_inc(y_copied, 1)
            act.sem_inc(y_saved, 16)
            mixer_act(act)
            wait_out(act, "out", 1, TT - 1)
            for t in range(TT):
                nc.scalar.activation(bank[:, 2 * t:2 * t + 2].rearrange("p a b -> p (a b)"), resid[:, t], ACT.Square,
                                     accum_out=ss[:, t:t + 1]).then_inc(sq_done, 1)
            act.wait_ge(rms_ready, 1)
            nc.scalar.activation(rstd, ss, ACT.Sqrt).then_inc(rms_ready, 1)
            act.wait_ge(h2_ready, TT)
            act.dma_start(h2_rows, h2).then_inc(h2_saved, 16)
            for k in range(KD):
                act.wait_ge(h2t_psum, k + 1)
                nc.scalar.activation(h2t[:, k], bank[:, k], ACT.Copy).then_inc(h2t_copied, 1)
            act.wait_ge(top_found, 1)
            nc.scalar.activation(wk, wk, ACT.Exp).then_inc(exp_done, 1)

            def sigmoid(n):
                act.wait_ge(glu_ready, n + 1)
                nc.scalar.activation(sig, glu, ACT.Sigmoid, scale=1.702).then_inc(sig_done, 1)

            def turn_hi(n, c):
                act.wait_ge(at_psum, n + 1)
                nc.scalar.activation(u_hi[:, c % 2, 0:256], bank[:, 6 + c % 2, 0:256], ACT.Copy).then_inc(at_hi, 1)

            def rows_hi(n):
                act.wait_ge(xt_psum, n + 1)
                nc.scalar.activation(t_hi[:, 0:2, :].rearrange("p a b -> p (a b)"),
                                     bank[:, 4:6].rearrange("p a b -> p (a b)"), ACT.Copy).then_inc(xt_hi, 1)

            def bias_half(n, e, half):
                act.dma_start(bias1[half], bias_d[e, :, 1024 * half:1024 * half + 1024]).then_inc(bias1_in[half], 16)

            def bias_out(n, e):
                act.dma_start(bias2, bias_d[e, :, HID:3072]).then_inc(bias2_in, 16)

            def run(passes):
                base = passes * STEPS
                g = first_granules(passes)
                for i in range(4):
                    split_hi(act, g[i])
                if not later(passes):
                    act.wait_ge(bias_saved, 16)
                    act.wait_ge(h2_saved, 16)
                    act.wait_ge(places_ready, 2)
                bias_half(passes * NE, 0, 0)
                bias_half(passes * NE, 0, 1)
                bias_out(passes * NE, 0)
                rows_hi(passes * NE)
                sigmoid(base)
                split_hi(act, g[4])
                split_hi(act, g[5])
                turn_hi(base, 0)

                def body(e, c, last):
                    n = e * 4 + base + c
                    if not (last and c == 3):
                        sigmoid(n + 1)
                    for g in step_granules(c, passes, e, last):
                        split_hi(act, g)
                    if not (last and c == 3):
                        turn_hi(n + 1, (c + 1) % 2)
                    if c == 0 and not last:
                        bias_half(0, e + 1, 0)
                    if c == 1 and not last:
                        act.wait_ge(h_done, e * 4 + base + 4)
                        rows_hi(e + passes * NE + 1)
                        bias_half(0, e + 1, 1)
                    if c == 3:
                        m = e + passes * NE
                        act.wait_ge(y_done, m + 1)
                        if not last:
                            bias_out(0, e + 1)
                        act.wait_ge(y_saved, m * 16 + 16)
                        nc.scalar.activation(ysb, bank[:, 2:4].rearrange("p a b -> p (a b)"), ACT.Copy)\
                            .then_inc(y_copied, 1)
                        act.wait_ge(y_copied, m + 2)
                        act.dma_start(y_rows[e], ysb).then_inc(y_saved, 16)

                expert_loop(act, body, passes)

            over_passes(act, run)
            more = act.value_load(flag_i[0:1, 0:1], min_val=0, max_val=SEQ)
            with act.If(more > CAP):
                act.wait_ge(comb_used, NPASS * TT * TOPK)
            for t in range(TT):
                act.wait_ge(comb_used, TOPK * (t + 1))
                nc.scalar.activation(bank[:, 2 * t:2 * t + 2].rearrange("p a b -> p (a b)"), resid[:, t], ACT.Square,
                                     accum_out=ss2[:, t:t + 1]).then_inc(sq2_done, 1)
            act.wait_ge(rms2_ready, 1)
            nc.scalar.activation(rstd2, ss2, ACT.Sqrt).then_inc(rms2_ready, 1)

        @block.vector
        def _(dve):
            link = Tally(dve, dve_own)
            mixer_dve(dve, link)
            nc.vector.memset(one3, 1.0).then_inc(one3_set, 1)
            dve.wait_ge(sq_done, TT)
            nc.vector.tensor_scalar(ss, ss, 1.0 / D, EPS, ALU.mult, ALU.add).then_inc(rms_ready, 1)
            dve.wait_ge(rms_ready, 2)
            link(nc.vector.reciprocal(rstd, rstd))
            dve.wait_ge(norm_in, 16)
            for t in range(TT):
                nc.vector.scalar_tensor_tensor(out=h2[:, t], in0=resid[:, t], scalar=rstd[:, t:t + 1], in1=wffn,
                                               op0=ALU.mult, op1=ALU.mult).then_inc(h2_ready, 1)
            dve.wait_ge(logit_psum, 1)
            dve.wait_ge(router_in, 32)
            link(nc.vector.tensor_tensor(logit, bank[:, 0, 0:TT * NE].rearrange("p (t e) -> p t e", t=TT),
                                         bc(rb, [(0, TT), (1, NE)]), ALU.add))
            for t in range(TT):
                link(nc.vector.max(mx8[:, t], logit[:, t]))
                link(nc.vector.max_index(ix8[:, t], mx8[:, t], logit[:, t]))
            nc.vector.tensor_tensor(wk, mx8[:, :, 0:TOPK], bc(mx8, [(8, TT), (0, TOPK)]), ALU.subtract)\
                .then_inc(top_found, 1)
            link(nc.vector.tensor_copy(ixf, ix8[:, :, 0:TOPK]))
            dve.wait_ge(late_in, 16)
            link(nc.vector.tensor_tensor(hot, bc(iota, [(0, TT * TOPK), (1, NE)]),
                                         bc(ixf, [(1, TT * TOPK), (0, NE)]), ALU.is_equal))
            nc.vector.tensor_reduce(mask, bc(hot, [(TOPK * NE, TT), (1, NE), (NE, TOPK)]), AX.X,
                                    ALU.add).then_inc(mask_ready, 1)
            dve.wait_ge(exp_done, 1)
            link(nc.vector.tensor_reduce(wsum, wk, AX.X, ALU.add))
            link(nc.vector.reciprocal(wrec, wsum))
            link(nc.vector.tensor_tensor(wk, wk, bc(wrec, [(1, TT), (0, TOPK)]), ALU.mult))
            dve.wait_ge(rank_psum, 1)
            for t in range(TT):
                link(nc.vector.tensor_tensor(hotr[:, t * TOPK:(t + 1) * TOPK], hot[:, t * TOPK:(t + 1) * TOPK],
                                             bc(bank[:, 1, t * NE:(t + 1) * NE], [(0, TOPK), (1, NE)]), ALU.mult))
            link(nc.vector.tensor_reduce(rk[:, 0], hotr, AX.X, ALU.add))
            link(nc.vector.tensor_scalar(rk[:, 1], rk[:, 0], float(CAP), None, ALU.is_ge))
            for b in range(2, NPASS):
                link(nc.vector.tensor_scalar(rk[:, 2], rk[:, 0], float(CAP * b), None, ALU.is_ge))
                link(nc.vector.tensor_tensor(rk[:, 1], rk[:, 1], rk[:, 2], ALU.add))
            ixf_flat = ixf.rearrange("p t k -> p (t k)")
            link(nc.vector.scalar_tensor_tensor(out=rk[:, 2], in0=rk[:, 1], scalar=-float(CAP), in1=rk[:, 0],
                                                op0=ALU.mult, op1=ALU.add))
            link(nc.vector.scalar_tensor_tensor(out=rk[:, 3], in0=rk[:, 2], scalar=float(NE), in1=ixf_flat,
                                                op0=ALU.mult, op1=ALU.add))
            link(nc.vector.scalar_tensor_tensor(out=addr[:, 0], in0=rk[:, 1], scalar=float(NE * P), in1=rk[:, 3],
                                                op0=ALU.mult, op1=ALU.add))
            nc.vector.tensor_copy(place_i, addr[:, 0]).then_inc(places_ready, 1)
            link(nc.vector.scalar_tensor_tensor(out=addr[:, 1], in0=ixf_flat, scalar=float(P), in1=rk[:, 2],
                                                op0=ALU.mult, op1=ALU.add))
            for b in range(NPASS):
                link(nc.vector.scalar_tensor_tensor(out=wk_pass[:, b], in0=rk[:, 1], scalar=float(b),
                                                    in1=wk.rearrange("p t k -> p (t k)"), op0=ALU.is_equal,
                                                    op1=ALU.mult))
            nc.vector.tensor_copy(slot_i, addr[:, 1]).then_inc(places_ready, 1)
            link(nc.vector.tensor_reduce(longest[:, 0:1], bank[:, 1, TT * NE:(TT + 1) * NE], AX.X, ALU.max))
            nc.vector.tensor_copy(flag_i, longest[:, 0:1]).then_inc(flag_ready, 1)

            def gate(n, c):
                hid = bank[:, c % 2].rearrange("p (n two) -> p two n", two=2)
                dve.wait_ge(h_done, n + 1)
                nc.vector.tensor_scalar(glu, hid[:, 0], 7.0, None, ALU.min).then_inc(glu_ready, 1)
                nc.vector.tensor_scalar(lin, hid[:, 1], 7.0, -7.0, ALU.min, ALU.max).then_inc(lin_ready, 1)
                dve.wait_ge(lin_ready, n + 1)
                dve.wait_ge(sig_done, n + 1)
                nc.vector.scalar_tensor_tensor(out=prod, in0=lin, scalar=1.0, in1=sig, op0=ALU.add, op1=ALU.mult)\
                    .then_inc(prod_ready, 1)
                dve.wait_ge(prod_ready, n + 1)
                nc.vector.tensor_tensor(act_t[c % 2], prod, glu, ALU.mult).then_inc(act_ready, 1)

            def turn_lo(n, c):
                dve.wait_ge(at_hi, n + 1)
                nc.vector.tensor_tensor(u_lo[:, c % 2, 0:256], bank[:, 6 + c % 2, 0:256],
                                        u_hi[:, c % 2, 0:256].bitcast(F32), ALU.subtract).then_inc(at_lo, 1)

            def rows_lo(n):
                dve.wait_ge(xt_hi, n + 1)
                nc.vector.tensor_tensor(t_lo[:, 0:2, :].rearrange("p a b -> p (a b)"),
                                        bank[:, 4:6].rearrange("p a b -> p (a b)"),
                                        t_hi[:, 0:2, :].rearrange("p a b -> p (a b)").bitcast(F32),
                                        ALU.subtract).then_inc(xt_lo, 1)

            def run(passes):
                base = passes * STEPS
                g = first_granules(passes)
                for i in range(4):
                    split_lo(dve, g[i])
                rows_lo(passes * NE)
                gate(base, 0)
                split_lo(dve, g[4])
                split_lo(dve, g[5])
                turn_lo(base, 0)

                def body(e, c, last):
                    n = e * 4 + base + c
                    if not (last and c == 3):
                        gate(n + 1, (c + 1) % 2)
                    for g in step_granules(c, passes, e, last):
                        split_lo(dve, g)
                    if not (last and c == 3):
                        turn_lo(n + 1, (c + 1) % 2)
                    if c == 1 and not last:
                        rows_lo(e + passes * NE + 1)

                expert_loop(dve, body, passes)
                for j in range(TT * TOPK):
                    t = j // TOPK
                    done = passes * TT * TOPK + j
                    dve.wait_ge(comb_in[j % 8], (passes * 2 + j // 8 + 1) * 16)
                    if j or later(passes):
                        dve.wait_ge(comb_used, done)
                    nc.vector.scalar_tensor_tensor(
                        out=resid[:, t], in0=raw[:, (j % 8) // 2, 1024 * (j % 2):1024 * (j % 2) + 1024],
                        scalar=wk_pass[:, passes, j:j + 1], in1=resid[:, t], op0=ALU.mult, op1=ALU.add)\
                        .then_inc(comb_used, 1)

            over_passes(dve, run)
            dve.wait_ge(sq2_done, TT)
            nc.vector.tensor_scalar(ss2, ss2, 1.0 / D, EPS, ALU.mult, ALU.add).then_inc(rms2_ready, 1)
            dve.wait_ge(rms2_ready, 2)
            link(nc.vector.reciprocal(rstd2, rstd2))
            dve.wait_ge(fin_in, 16)
            for t in range(TT):
                nc.vector.scalar_tensor_tensor(out=resid[:, t], in0=resid[:, t], scalar=rstd2[:, t:t + 1],
                                               in1=wfin, op0=ALU.mult, op1=ALU.mult).then_inc(out_ready, 1)

        @block.tensor
        def _(pe):
            mixer_pe(pe)
            for k in range(KD):
                for t in range(TT):
                    if k == 0:
                        pe.wait_ge(h2_ready, t + 1)
                    m = nc.tensor.transpose(bank[:, k, t * P:(t + 1) * P], h2[:, t, k * P:(k + 1) * P], ident)
                m.then_inc(h2t_psum, 1)
            pe.wait_ge(h2t_copied, KD)
            pe.wait_ge(router_in, 32)
            for t in range(TT):
                for k in range(KD):
                    m = nc.tensor.matmul(bank[:, 0, t * NE:(t + 1) * NE], h2t[:, k, t * P:(t + 1) * P], rw[:, k],
                                         start=(k == 0), stop=(k == KD - 1))
            m.then_inc(logit_psum, 1)
            pe.wait_ge(mask_ready, 1)
            pe.wait_ge(late_in, 16)
            for t in range(TT):
                for j in range(t):
                    nc.tensor.matmul(bank[:, 1, t * NE:(t + 1) * NE], ones, mask[:, j], start=(j == 0), stop=False)
                nc.tensor.matmul(bank[:, 1, t * NE:(t + 1) * NE], tri_lt, mask[:, t], start=(t == 0), stop=True)
            for t in range(TT):
                m = nc.tensor.matmul(bank[:, 1, TT * NE:(TT + 1) * NE], ones, mask[:, t], start=(t == 0),
                                     stop=(t == TT - 1))
            m.then_inc(rank_psum, 1)

            def rows(n):
                pe.wait_ge(xg_in, n * 16 + 16)
                if not (isinstance(n, int) and n == 0):
                    pe.wait_ge(xt_lo, n)
                for k in range(KD):
                    m = nc.tensor.transpose(bank[:, 4 + k // 4, (k % 4) * P:(k % 4 + 1) * P], xg[:, k], ident)
                m.then_inc(xt_psum, 1)

            def hidden(g0, g1, c, n, expert):
                hid = bank[:, c % 2]
                if not (isinstance(n, int) and n < 2):
                    pe.wait_ge(act_ready, n - 1)
                for k in range(KD):
                    g = (g0, g1)[k // 4]
                    if k % 4 == 0:
                        pe.wait_ge(lo_done, g.n + 1)
                    cols = slice(512 * (k % 4), 512 * (k % 4) + 512)
                    rows_k = slice(k * P % 512, k * P % 512 + P)
                    m = product(hid, t_hi[:, k // 4, rows_k], t_lo[:, k // 4, rows_k], whi[:, g.slot, cols],
                                wlo[:, g.slot, cols], k == 0, False)
                    if k % 4 == 3:
                        m.then_inc(granule_used, 1)
                pe.wait_ge(bias1_in[c // 2], expert * 16 + 16)
                nc.tensor.matmul(hid, one3, bias1[c // 2][:, 512 * (c % 2):512 * (c % 2) + 512],
                                 start=False, stop=True).then_inc(h_done, 1)

            def turn(n, c):
                pe.wait_ge(act_ready, n + 1)
                for j in range(2):
                    m = nc.tensor.transpose(bank[:, 6 + c % 2, j * P:(j + 1) * P], act_t[c % 2][:, j * P:(j + 1) * P],
                                            ident)
                m.then_inc(at_psum, 1)

            def outputs(g, n, c, expert):
                pe.wait_ge(at_lo, n + 1)
                if c == 0:
                    pe.wait_ge(y_copied, expert + 1)
                pe.wait_ge(lo_done, g.n + 1)
                for j in range(2):
                    for h in range(2):
                        cols = slice(1024 * j + 512 * h, 1024 * j + 512 * h + 512)
                        m = product(bank[:, 2 + h], u_hi[:, c % 2, j * P:(j + 1) * P],
                                    u_lo[:, c % 2, j * P:(j + 1) * P], whi[:, g.slot, cols], wlo[:, g.slot, cols],
                                    c == 0 and j == 0, False)
                m.then_inc(granule_used, 1)
                if c == 3:
                    pe.wait_ge(bias2_in, expert * 16 + 16)
                    for h in range(2):
                        m = nc.tensor.matmul(bank[:, 2 + h], one3, bias2[:, 512 * h:512 * h + 512], start=False,
                                             stop=True)
                    m.then_inc(y_done, 1)

            def run(passes):
                base = passes * STEPS
                g = first_granules(passes)
                rows(passes * NE)
                pe.wait_ge(one3_set, 1)
                pe.wait_ge(xt_lo, passes * NE + 1)
                hidden(g[0], g[1], 0, base, passes * NE)
                hidden(g[2], g[3], 1, base + 1, passes * NE)
                turn(base, 0)

                def body(e, c, last):
                    n = e * 4 + base + c
                    expert = e + passes * NE
                    if c == 1 and not last:
                        rows(expert + 1)
                    if not (last and c >= 2):
                        first = MIX_GRANULES + 3 * c + 4
                        ga, gb = ((Granule(first, passes, e), Granule(first + 1, passes, e)) if not last else
                                  (Granule(first + 12 * (NE - 1), passes), Granule(first + 12 * (NE - 1) + 1, passes)))
                        if c == 2:
                            pe.wait_ge(xt_lo, expert + 2)
                        hidden(ga, gb, (c + 2) % 4, n + 2, expert if c < 2 else expert + 1)
                    if not (last and c == 3):
                        turn(n + 1, (c + 1) % 2)
                    outputs(step_granules(c, passes, e, last)[0], n, c, expert)

                expert_loop(pe, body, passes)

            over_passes(pe, run)




_INS = ['x', 'w_in', 'rel_bias', 'w_branch_attn', 'conv_w', 'conv_b', 'dt_bias', 'a_log', 'd_skip', 'ssm_norm_w',
        'w_branch_ssm', 'gate_bias', 'w_out', 'norm_mix', 'norm_ffn', 'router_w', 'router_b', 'w1', 'b1', 'w2', 'b2',
        'norm_final']
_OUTS = [((1, SEQ, D), 'float32')]


def constants():
    import numpy as np
    p, f = np.arange(P)[:, None], np.arange(P)[None, :]
    return np.concatenate([p == f, p <= f, p > f, np.ones((P, P)), p < f, np.broadcast_to(np.arange(NE), (P, NE))],
                          axis=1).astype(np.float32)


def bucket_rows():
    import math
    import numpy as np
    hot = np.zeros((NBK + 1, 3 * BR + NH_A), np.float32)
    for g, (window, dilation) in enumerate(GROUPS):
        for j in range(BR):
            delta = 255 - j
            if g == 2:
                valid, dist = delta >= 0 and delta % 4 == 0, delta // 4
            else:
                valid, dist = 0 <= delta <= window // dilation, delta
            if not valid:
                hot[NBK, g * BR + j] = -BIG
                continue
            dist *= dilation
            half = NBK // 2
            large = half + int(np.float32(np.log(np.float32(max(dist, half) / half)) / np.float32(
                math.log(MAX_DIST / half)) * np.float32(NBK - half)))
            hot[dist if dist < half else min(large, NBK - 1), g * BR + j] = 1.0
    hot[NBK, 3 * BR:] = 1.0
    return hot


def kernel(**inputs):
    import numpy as _np
    import concourse.bacc as _bacc
    from concourse import mybir as _mybir
    from concourse.bass_utils import run_bass_kernel_spmd as _run

    nc = _bacc.Bacc("TRN2", target_bir_lowering=False, num_devices=1)
    arrays, args = {}, []
    given = [(name, inputs[name]) for name in _INS] + [("consts", constants()), ("buckets", bucket_rows())]
    for name, a in given:
        a = _np.ascontiguousarray(a)
        arrays[f"in_{name}_dram"] = a
        args.append(nc.dram_tensor(f"in_{name}_dram", a.shape, _mybir.dt.from_np(a.dtype), kind="ExternalInput").ap())
    for i, (shape, dtype) in enumerate(_OUTS):
        dt = _mybir.dt.from_np(_np.dtype(dtype))
        args.append(nc.dram_tensor(f"out_{i}_dram", shape, dt, kind="ExternalOutput").ap())
    build(nc, *args)
    r = _run(nc, [arrays], core_ids=[0])
    got = tuple(r.results[0][f"out_{i}_dram"] for i in range(len(_OUTS)))
    return got[0]
```

```python
from contextlib import ExitStack

import concourse.bass as bass
from concourse import mybir

F32 = mybir.dt.float32
F32R = mybir.dt.float32r
BF16 = mybir.dt.bfloat16
I32 = mybir.dt.int32
U32 = mybir.dt.uint32
ALU = mybir.AluOpType
ACT = mybir.ActivationFunctionType
AX = mybir.AxisListType

P = 128
SEQ, D = 512, 1024
TT = SEQ // P
KD = D // P
EPS = 1e-5
NE, TOPK = 32, 4
HID = 2 * D
CAP = 128
NPASS = SEQ // CAP
BIG = 1e30

RING = 4
GW = 2048
MIX_GRANULES = 60
STEPS = 4 * NE
PASS_GRANULES = 3 * STEPS

ARENA = 15488

C_ID, C_LE, C_GT, C_ONE, C_END = 0, 128, 256, 384, 512
C_LT, C_IOTA, C_ALL = 512, 640, 672

NG, HPG, HEAD_DIM = 3, 8, 64
NH_A, NHS, NSG = 24, 32, 4
CONV_WIDTH = 4
GROUPS = ((128, 1), (512, 4), (2048, 16))
NBK, MAX_DIST = 32, 2048
BR = 384
SKEW = P * (BR + 1)
COL_Z = 3 * NH_A * HEAD_DIM
COL_X = COL_Z + 2 * D
COL_B = COL_X + 2 * D
COL_DT = COL_B + 2 * 512
COL_G = COL_DT + NHS


def bc(ap, pairs):
    return bass.AP(ap.tensor, ap.offset, [list(ap.ap[0])] + [list(q) for q in pairs])


class Tally:

    def __init__(self, eng, sem):
        self.eng, self.sem, self.n = eng, sem, 0

    def __call__(self, ins):
        ins.then_inc(self.sem, 1)
        self.n += 1
        self.eng.wait_ge(self.sem, self.n)


def build(nc, x, w_in, rel_bias, w_branch_attn, conv_w, conv_b, dt_bias, a_log, d_skip, ssm_norm_w,
          w_branch_ssm, gate_bias, w_out, norm_mix, norm_ffn, router_w, router_b, w1, b1, w2, b2, norm_final, consts,
          buckets, out):
    with ExitStack() as ctx:
        def sb(name, shape, dt=F32):
            return ctx.enter_context(nc.sbuf_tensor(name, shape, dt))

        def sem(name):
            return ctx.enter_context(nc.semaphore(name))

        def dram(name, shape, dt=F32):
            return nc.dram_tensor(name, shape, dt, kind="Internal").ap()

        raw = sb("raw", [P, RING, GW])
        whi = sb("whi", [P, RING, GW], F32R)
        wlo = sb("wlo", [P, RING, GW], F32R)
        t_hi = sb("t_hi", [P, KD, SEQ], F32R)
        t_lo = sb("t_lo", [P, KD, SEQ], F32R)
        u_hi = sb("u_hi", [P, 4, SEQ], F32R)
        u_lo = sb("u_lo", [P, 4, SEQ], F32R)
        cst = sb("cst", [P, C_END])
        arena = sb("arena", [P, ARENA])
        bank = ctx.enter_context(nc.psum_tensor("bank", [P, 8, 512], F32))
        ident, tri_le, tri_gt = cst[:, C_ID:C_LE], cst[:, C_LE:C_GT], cst[:, C_GT:C_ONE]
        ones = cst[:, C_ONE:C_END]

        class Region:

            def __init__(self, first, end):
                self.at, self.end = first, end

            def __call__(self, *dims, dt=F32, parts=P):
                n = 1
                for d in dims:
                    n *= d
                words = n if dt != BF16 else (n + 1) // 2
                ap = arena[0:parts, self.at:self.at + words]
                self.at += words
                assert self.at <= self.end
                if dt != F32:
                    ap = ap.bitcast(dt)
                if len(dims) > 1:
                    names = "abcd"[:len(dims)]
                    ap = ap.rearrange(f"p ({' '.join(names)}) -> p {' '.join(names)}",
                                      **dict(zip(names[1:], dims[1:])))
                return ap

        keep = Region(0, 4096 + 960)
        resid = keep(TT, D)
        wk = keep(TT, TOPK)
        wk_pass = keep(NPASS, TT * TOPK)
        slot_i = keep(TT * TOPK, dt=I32)
        place_i = keep(TT * TOPK, dt=I32)
        tokc = keep(TT, dt=I32)
        flag_i = keep(1, dt=I32)
        idx = keep(1, dt=I32)
        ss, rstd, ss2, rstd2, wsum, wrec, longest = [keep(4) for _ in range(7)]
        table = keep(NPASS, NE, dt=I32)
        one3 = keep(P, dt=BF16, parts=3)
        route = Region(5056, ARENA)
        h2 = route(TT, D)
        h2t = route(KD, SEQ)
        wffn = h2t[:, 0:2].rearrange("p a b -> p (a b)")
        rw = route(KD, NE)
        rb = route(NE)
        logit = route(TT, NE)
        mx8 = route(TT, 8)
        ix8 = route(TT, 8, dt=U32)
        ixf = route(TT, TOPK)
        mask = route(TT, NE)
        hot = route(TT * TOPK, NE)
        hotr = route(TT * TOPK, NE)
        late = route(160)
        tri_lt, iota = late[:, 0:P], late[:, C_IOTA - C_LT:C_ALL - C_LT]
        rk = route(4, TT * TOPK)
        addr = route(2, TT * TOPK)
        expert = Region(5056, ARENA)
        xg = expert(KD, P)
        ysb = expert(D)
        glu, lin, sig, prod = [expert(256) for _ in range(4)]
        act_t = [expert(256) for _ in range(2)]
        bias1 = [expert(1024, dt=BF16, parts=3) for _ in range(2)]
        bias2 = expert(1024, dt=BF16, parts=3)
        wfin = expert(D)
        h2_d = dram("h2_d", (SEQ, D))
        tok_d = dram("tok_d", (NPASS * P * NE, 1), I32)
        y_d = dram("y_d", (NE * P, D))
        bias_d = dram("bias_d", (NE, 3, 3072), BF16)

        raw_in = [sem(f"raw_in{s}") for s in range(RING)]
        hi_done, lo_done, granule_used = sem("hi_done"), sem("lo_done"), sem("granule_used")
        const_in, bias_raw_in, bias_split, bias_saved = (sem("const_in"), sem("bias_raw_in"),
                                                         sem("bias_split"), sem("bias_saved"))
        tok_zeroed, zero_set, ids_set = sem("tok_zeroed"), sem("zero_set"), sem("ids_set")
        x_in, sq_done, rms_ready, norm_in, h2_ready, h2_saved = (sem("x_in"), sem("sq_done"), sem("rms_ready"),
                                                       sem("norm_in"), sem("h2_ready"), sem("h2_saved"))
        h2t_psum, h2t_copied, logit_psum, router_in = (sem("h2t_psum"), sem("h2t_copied"),
                                                       sem("logit_psum"), sem("router_in"))
        top_found, exp_done, mask_ready, rank_psum = (sem("top_found"), sem("exp_done"), sem("mask_ready"),
                                                      sem("rank_psum"))
        places_ready, tok_saved, table_in, flag_ready = (sem("places_ready"), sem("tok_saved"),
                                                         sem("table_in"), sem("flag_ready"))
        xg_in, xt_psum, xt_hi, xt_lo = (sem("xg_in"), sem("xt_psum"), sem("xt_hi"),
                                                   sem("xt_lo"))
        bias1_in = [sem("bias1a_in"), sem("bias1b_in")]
        bias2_in = sem("bias2_in")
        h_done, glu_ready, lin_ready, sig_done, prod_ready, act_ready = (
            sem("h_done"), sem("glu_ready"), sem("lin_ready"), sem("sig_done"), sem("prod_ready"), sem("act_ready"))
        at_psum, at_hi, at_lo = sem("at_psum"), sem("at_hi"), sem("at_lo")
        y_done, y_copied, y_saved = sem("y_done"), sem("y_copied"), sem("y_saved")
        comb_in = [sem(f"comb_in{i}") for i in range(8)]
        comb_used = sem("comb_used")
        sq2_done, rms2_ready, fin_in, out_ready, out_saved = (
            sem("sq2_done"), sem("rms2_ready"), sem("fin_in"), sem("out_ready"),
            sem("out_saved"))
        dve_own = sem("dve_own")
        late_in, one3_set = sem("late_in"), sem("one3_set")

        x_t = Region(0, 4096)(TT, D)
        early = Region(4096, ARENA)
        hotb = early(3 * BR + NH_A, parts=NBK + 1)
        rowb = early(3, BR, parts=HPG)
        bfull = early(3072, parts=NE)
        bpart = early(3, 3072, dt=BF16, parts=NE)
        zero_i = early(P, dt=I32)
        ldrows = early(P)
        ldrows2 = early(P)
        dtw_raw = Region(0, 4096)(KD, NHS)
        att = Region(0, ARENA)
        q_t = [att(4, SEQ) for _ in range(NG)]
        k_t = att(4, SEQ)
        v_t = att(TT, 512)
        bias_t = att(HPG, 256)
        prob_t = [att(TT, 256) for _ in range(2)]
        pturn = att(7, P)
        m_all = att(NG, TT, HPG)
        d_all = att(NG, TT, HPG)
        merge = Region(6144, ARENA)
        m_row = merge(NG, SEQ, parts=HPG)
        d_row = merge(NG, SEQ, parts=HPG)
        e_row = merge(NG, SEQ, parts=HPG)
        top_row = merge(SEQ, parts=HPG)
        z_row = merge(SEQ, parts=HPG)
        ssd = Region(0, ARENA)
        b_t = ssd(SEQ)
        c_t = ssd(SEQ)
        b_tok = ssd(TT, P)
        cbm = ssd(TT, P)
        xs = ssd(TT, 512)
        zs = ssd(TT, 512)
        conv_t = [ssd(SEQ) for _ in range(2)]
        ramp = ssd(HPG, P)
        dec = [ssd(HPG, P) for _ in range(2)]
        xd = [conv_t[0], conv_t[1]] + [ssd(512) for _ in range(2)]
        xdd = ssd(512)
        state = ssd(512)
        y_t = ssd(512)
        y_turn = [ssd(SEQ) for _ in range(2)]
        dts = ssd(TT, NHS)
        a_d = ssd(TT, NHS)
        dec3 = ssd(3, TT, NHS)
        dskip = ssd(NHS)
        a_neg = ssd(NHS)
        dtb = ssd(NHS)
        sp = [y_turn[0][:, i * 128:(i + 1) * 128].rearrange("p (t h) -> p t h", t=TT) for i in range(4)]
        gates = Region(4096, 4096 + 8192)(2, KD, SEQ)
        y_back = [Region(0, 2048)(4, SEQ), Region(2048, 4096)(4, SEQ), Region(12288, 14336)(4, SEQ)]
        small = sb("small", [P, 176])
        msm = small[:, 0:4], small[:, 4:8]
        ms, mrstd = msm
        nm_t = small[:, 8:12], small[:, 148:152]
        gss, grstd = small[:, 12:16], small[:, 16:20]
        dt_rows = q_t[1][0:NHS, 3]
        dt_raw = small[:, 20:148].rearrange("p (t h) -> p t h", t=TT)
        cols = sb("cols", [P, 160])
        col_cw = lambda j, f: cols[:, 24 * j + f:24 * j + f + 1]
        col_cb = lambda f: cols[:, 96 + f:97 + f]
        col_nm = lambda k: cols[:, 120 + k:121 + k]
        col_gb = lambda f: cols[:, 128 + f:129 + f]
        col_sn = lambda f: cols[:, 144 + f:145 + f]

        rel_d = dram("rel_d", (NG * HPG * SKEW, 1))
        yt_d = dram("yt_d", (NSG, 4, P, SEQ))

        cols_in, cols_psum, cols_ready = sem("cols_in"), sem("cols_psum"), sem("cols_ready")
        xm_in, msq_done, mrms, xn_ready, ht_psum, ht_hi, ht_lo = (
            [sem("xm_in0"), sem("xm_in1")], sem("msq_done"), sem("mrms"), sem("xn_ready"), sem("ht_psum"), sem("ht_hi"), sem("ht_lo"))
        buckets_in, table_rows_in, rel_psum, rel_copied, rel_saved, bias_in = (
            sem("buckets_in"), sem("table_rows_in"), sem("rel_psum"), sem("rel_copied"), sem("rel_saved"),
            sem("bias_in"))
        dtw_in, dtw_hi, dtw_lo, dt_psum, dt_out = (sem("dtw_in"), sem("dtw_hi"), sem("dtw_lo"), sem("dt_psum"),
                                                   sem("dt_out"))
        tile_done, act_out, dve_out = sem("tile_done"), sem("act_out"), sem("dve_out")
        s_psum, s_out, neg_ready, p_ready, pt_psum, pt_out, u_psum, u_out = (
            sem("s_psum"), sem("s_out"), sem("neg_ready"), sem("p_ready"), sem("pt_psum"), sem("pt_out"),
            sem("u_psum"), sem("u_out"))
        row_psum, row_out, row_less, row_exp, share_ready, share_psum, share_used = (
            sem("row_psum"), sem("row_out"), sem("row_less"), sem("row_exp"), sem("share_ready"),
            sem("share_psum"), sem("share_used"))
        attn_sum, attn_hi, attn_lo = sem("attn_sum"), sem("attn_hi"), sem("attn_lo")
        dtc_in, sp_abs, sp_exp, sp_one, sp_ln, a_ready, cs_psum, cs_exp = (
            sem("dtc_in"), sem("sp_abs"), sem("sp_exp"), sem("sp_one"), sem("sp_ln"), sem("a_ready"), sem("cs_psum"),
            sem("cs_exp"))
        conv_on, conv_silu = sem("conv_on"), sem("conv_silu")
        xs_psum, xs_out, bt_psum, bt_out, cb_psum, cb_out = (
            sem("xs_psum"), sem("xs_out"), sem("bt_psum"), sem("bt_out"), sem("cb_psum"), sem("cb_out"))
        ramp_ready, seg_psum, dec_ready, mat_ready, xd_ready, xdd_ready = (
            sem("ramp_ready"), sem("seg_psum"), sem("dec_ready"), sem("mat_ready"), sem("xd_ready"),
            sem("xdd_ready"))
        off_psum, st_psum, diag_psum, off_used, st_used, y_chunk = (
            sem("off_psum"), sem("st_psum"), sem("diag_psum"), sem("off_used"), sem("st_used"),
            sem("y_chunk"))
        skip_ready, skip_used = sem("skip_ready"), sem("skip_used")
        gsq_done, grms, yn_ready, yt_psum, yt_out = (
            sem("gsq_done"), sem("grms"), sem("yn_ready"), sem("yt_psum"), sem("yt_out"))
        yt_saved = [sem("yt_saved0"), sem("yt_saved1")]
        yb_in = [sem(f"yb_in{i}") for i in range(3)]
        yb_hi, yb_lo = sem("yb_hi"), sem("yb_lo")
        merged_f, merged_hi, merged_lo = sem("merged_f"), sem("merged_hi"), sem("merged_lo")

        panels = []
        for g in range(NG):
            panels += [("q", g, 4, 2, "act"), ("k", g, 4, 2, "act"), ("v", g, 4, 2, "act")]
        for g in range(NSG):
            panels += [("bc", g, 2, 1, "dve"), ("xs", g, 4, 2, "dve"), ("z", g, 4, 2, "act")]
        panels += [("gate", i, 4, 2, "act") for i in range(4)]
        panels += [("attn", h, 4, 1, "dve") for h in range(2)]
        panels += [("ssm", 2 * g + h, 4, 1, "dve" if g == NSG - 1 else None) for g in range(NSG) for h in range(2)]
        panels += [("out", h, 4, 2, "dve") for h in range(2)]

        first_of, ready_at, out_at, landed_at = {}, {}, {}, {}
        n_granule, n_tile, n_out, n_slot = 0, 0, {"act": 0, "dve": 0, None: 0}, [0] * RING
        for name, g, tiles, granules, owner in panels:
            first_of[name, g] = n_granule
            for j in range(tiles):
                if j < tiles - 1:
                    n_tile += 1
                    ready_at[name, g, j] = (tile_done, n_tile)
                else:
                    ready_at[name, g, j] = (granule_used, n_granule + granules)
                n_out[owner] += 1
                out_at[name, g, j] = (act_out if owner == "act" else dve_out, n_out[owner])
            for _ in range(granules):
                n_slot[n_granule % RING] += 2 if name == "bc" else 1
                landed_at[n_granule] = 16 * n_slot[n_granule % RING]
                n_granule += 1
        assert n_granule == MIX_GRANULES and MIX_GRANULES % RING == 0
        extra = [n_slot[s] - MIX_GRANULES // RING for s in range(RING)]

        def panel_granules(i):
            name, g, tiles, granules, owner = panels[i]
            return [Granule(first_of[name, g] + j) for j in range(granules)]

        order = {(p[0], p[1]): i for i, p in enumerate(panels)}

        def wait_tile(eng, *key):
            eng.wait_ge(*ready_at[key])

        def wait_out(eng, *key):
            eng.wait_ge(*out_at[key])

        def group_tokens(row, g, t=None):
            v = row.rearrange("p (t i) -> p t i" if g == 0 else "p (i t) -> p t i", t=TT)
            return v if t is None else v[:, t]

        def in_tiles(ap):
            return ap.rearrange("p (t i) -> p t i", t=TT)

        def mixer_loads(sp):
            w_in_v = w_in.rearrange("a (k p) n -> p (a k) n", p=P)
            wba_v = w_branch_attn.rearrange("a (k p) n -> p (a k) n", p=P)
            wbs_v = w_branch_ssm.rearrange("a (k p) n -> p (a k) n", p=P)
            wo_v = w_out.rearrange("a (k p) n -> p (a k) n", p=P)
            sp.dma_start(cst[:], consts[:, 0:C_END]).then_inc(const_in, 16)
            sp.dma_start(ldrows[0:96], conv_w.rearrange("a j (f p) -> (a j f) p", p=P)).then_inc(cols_in, 16)
            sp.dma_start(ldrows[96:120], conv_b.rearrange("a (f p) -> (a f) p", p=P)).then_inc(cols_in, 16)
            sp.dma_start(ldrows2[0:8], norm_mix.rearrange("a (f p) -> (a f) p", p=P)).then_inc(cols_in, 16)
            sp.dma_start(ldrows2[8:24], gate_bias.rearrange("a (f p) -> (a f) p", p=P)).then_inc(cols_in, 16)
            sp.dma_start(ldrows2[24:40], ssm_norm_w.rearrange("a (f p) -> (a f) p", p=P)).then_inc(cols_in, 16)
            for half in range(2):
                sp.dma_start(x_t[:, 2 * half:2 * half + 2], x_rows[:, 2 * half:2 * half + 2]).then_inc(xm_in[half], 16)
            sp.dma_start(hotb, buckets).then_inc(buckets_in, 16)
            def load_panel(i):
                name, g, tiles, granules, owner = panels[i]
                for h, gr in enumerate(panel_granules(i)):
                    if gr.reused:
                        sp.wait_ge(lo_done, gr.n - RING + 1)
                    dst = raw[:, gr.slot].rearrange("p (k n) -> p k n", k=8 if name == "bc" else 4)
                    ks = slice(4 * h, 4 * h + 4)
                    if name == "bc":
                        for part in range(2):
                            col = COL_B + 512 * part + P * g
                            sp.dma_start(dst[:, :, P * part:P * part + P], w_in_v[:, :, col:col + P])\
                                .then_inc(raw_in[gr.slot], 16)
                        continue
                    if name == "attn":
                        src = wba_v[:, 0:4, 512 * g:512 * g + 512]
                    elif name == "ssm":
                        src = wbs_v[:, 4 * (g // 2):4 * (g // 2) + 4, 512 * (g % 2):512 * (g % 2) + 512]
                    elif name == "out":
                        src = wo_v[:, ks, 512 * g:512 * g + 512]
                    else:
                        col = {"q": 0, "k": 1536, "v": 3072, "z": COL_Z, "xs": COL_X, "gate": COL_G}[name] + 512 * g
                        src = w_in_v[:, ks, col:col + 512]
                    sp.dma_start(dst, src).then_inc(raw_in[gr.slot], 16)

            def spill(g):
                for f in range(4):
                    n = 4 * g + f
                    sp.wait_ge(yt_out, n + 1)
                    sp.dma_start(yt_d[g, f], y_turn[f % 2]).then_inc(yt_saved[f % 2], 16)

            load_panel(0)
            sp.wait_ge(buckets_in, 16)
            sp.dma_start(hotb[0:NBK, 3 * BR:], rel_bias).then_inc(table_rows_in, 16)
            sp.dma_start(bfull[:, 0:HID], b1[0]).then_inc(bias_raw_in, 16)
            sp.dma_start(bfull[:, HID:3072], b2[0]).then_inc(bias_raw_in, 16)
            load_panel(1)
            sp.wait_ge(ht_psum, KD)
            sp.dma_start(dtw_raw, w_in_v[:, :, COL_DT:COL_DT + NHS]).then_inc(dtw_in, 16)
            sp.wait_ge(zero_set, 1)
            sp.dma_start(tok_d.rearrange("(p n) a -> p (n a)", p=P), zero_i).then_inc(tok_zeroed, 16)
            sp.wait_ge(rel_copied, NG)
            load_panel(2)
            for g in range(NG):
                sp.dma_start(bass.AP(rel_d.tensor, g * HPG * SKEW, [[SKEW, HPG], [BR + 1, P], [1, BR]]),
                             bc(rowb[:, g], [(0, P), (1, BR)])).then_inc(rel_saved, 16)
            sp.wait_ge(bias_split, 5)
            sp.dma_start(bias_d, bpart).then_inc(bias_saved, 16)
            sp.wait_ge(rel_saved, 16 * NG)
            sp.wait_ge(bias_saved, 16)
            sp.wait_ge(tok_zeroed, 16)
            for g in range(NG):
                if g:
                    sp.wait_ge(s_out, HPG * g)
                off, n = (127, 256) if g == 0 else (255, P)
                sp.dma_start(bias_t[:, :, 0:n], bass.AP(rel_d.tensor, g * HPG * SKEW + off, [[BR, P], [SKEW, HPG], [1, n]]))\
                    .then_inc(bias_in, 16)
                for i in range(3 * g + 2, 3 * g + 5):
                    if i > 2:
                        load_panel(i)
            i = 3 * NG + 2
            for g in range(NSG):
                if g == 0:
                    sp.wait_ge(attn_hi, 4)
                    sp.wait_ge(attn_lo, 4)
                    for ap, src in ((dskip, d_skip), (a_neg, a_log), (dtb, dt_bias)):
                        sp.dma_start(ap, src.broadcast_to([P, NHS])).then_inc(dtc_in, 16)
                for _ in range(3):
                    if i < order["gate", 0]:
                        load_panel(i)
                        i += 1
                if g:
                    spill(g - 1)
            load_panel(order["gate", 0])
            load_panel(order["gate", 1])
            spill(NSG - 1)
            for i in range(order["gate", 2], len(panels)):
                if i == order["gate", 2]:
                    for g in range(3):
                        if g == 0:
                            sp.wait_ge(yt_saved[0], 16 * 2 * NSG)
                            sp.wait_ge(yt_saved[1], 16 * 2 * NSG)
                        sp.dma_start(y_back[g], yt_d[g].rearrange("f p s -> p f s")).then_inc(yb_in[g], 16)
                load_panel(i)
                if i == order["ssm", 1]:
                    sp.wait_ge(yb_lo, 1)
                    sp.dma_start(y_back[0], yt_d[3].rearrange("f p s -> p f s")).then_inc(yb_in[0], 16)
            sp.wait_ge(yb_lo, NSG)
            sp.dma_start(resid, x_rows).then_inc(x_in, 16)

        w1_v = w1.rearrange("a e (k p) n -> (a e) p k n", p=P)
        w2_v = w2.rearrange("a e (k p) n -> (a e) p k n", p=P)
        y_rows = y_d.rearrange("(b p) d -> b p d", p=P)
        x_rows = x.rearrange("a (t p) d -> p (a t) d", p=P)
        out_rows = out.rearrange("a (t p) d -> p (a t) d", p=P)
        h2_rows = h2_d.rearrange("(t p) d -> p t d", p=P)

        class Granule:

            def __init__(self, first, passes=0, e=0):
                assert PASS_GRANULES % RING == 0 and 12 % RING == 0
                self.slot = first % RING
                self.n = first + passes * PASS_GRANULES + e * 12
                if first < MIX_GRANULES:
                    self.landed = landed_at[first]
                else:
                    turn = first // RING + passes * (PASS_GRANULES // RING) + e * (12 // RING)
                    self.landed = turn * 16 + 16 * extra[self.slot] + 16
                self.reused = first >= RING

        def split_hi(act, g):
            act.wait_ge(raw_in[g.slot], g.landed)
            if g.reused:
                act.wait_ge(granule_used, g.n - RING + 1)
            nc.scalar.activation(whi[:, g.slot], raw[:, g.slot], ACT.Copy).then_inc(hi_done, 1)

        def split_lo(dve, g):
            dve.wait_ge(hi_done, g.n + 1)
            nc.vector.tensor_tensor(wlo[:, g.slot], raw[:, g.slot], whi[:, g.slot].bitcast(F32),
                                    ALU.subtract).then_inc(lo_done, 1)

        def load(sp, g, src, shape):
            if g.reused:
                sp.wait_ge(lo_done, g.n - RING + 1)
            dst = raw[:, g.slot].rearrange("p (k n) -> p k n", k=shape)
            sp.dma_start(dst, src).then_inc(raw_in[g.slot], 16)

        def product(ps, a_hi, a_lo, b_hi, b_lo, start, stop):
            nc.tensor.matmul(ps, a_hi, b_hi, start=start, stop=False)
            nc.tensor.matmul(ps, a_hi, b_lo, start=False, stop=False)
            return nc.tensor.matmul(ps, a_lo, b_hi, start=False, stop=stop)

        def step_granules(c, passes, e, last):
            if not last:
                b0 = MIX_GRANULES + 6 + 3 * c
                return [Granule(b0, passes, e), Granule(b0 + 1, passes, e), Granule(b0 + 2, passes, e)]
            k = 4 * (NE - 1) + c
            if c == 0:
                b0 = MIX_GRANULES + 6 + 3 * k
                return [Granule(b0, passes), Granule(b0 + 1, passes), Granule(b0 + 2, passes)]
            return [Granule(MIX_GRANULES + PASS_GRANULES - 4 + c, passes)]

        def expert_loop(eng, body, passes):
            with eng.Fori(0, NE - 1) as e:
                for c in range(4):
                    body(e, c, False)
            for c in range(4):
                body(NE - 1, c, True)

        def over_passes(eng, run):
            run(0)
            eng.wait_ge(flag_ready, 1)
            more = eng.value_load(flag_i[0:1, 0:1], min_val=0, max_val=SEQ)
            with eng.If(more > CAP):
                if eng is nc.gpsimd:
                    for passes in range(1, NPASS):
                        run(passes)
                else:
                    with eng.Fori(1, NPASS) as passes:
                        run(passes)

        def first_granules(passes):
            return [Granule(MIX_GRANULES + i, passes) for i in range(6)]

        def later(passes):
            return not (isinstance(passes, int) and passes == 0)

        def conv_columns(g, j):
            return (16 + g, 20 + g, 4 * g, 4 * g + 1, 4 * g + 2, 4 * g + 3)[j]

        def conv_key(g, j):
            return ("bc", g, j) if j < 2 else ("xs", g, j - 2)

        def conv_bank(name, g, j):
            return 6 + j if name == "bc" else j

        def logits(g, n):
            b0 = 4 if n % 2 == 0 else 2
            return (bank[:, b0:b0 + 2].rearrange("p a (t k) -> p (a t) k", t=2) if g == 0 else
                    bank[:, b0].rearrange("p (t k) -> p t k", t=TT))

        def probs(g, n):
            p = prob_t[n % 2]
            return p if g == 0 else p[:, 0:2].rearrange("p a (b k) -> p (a b) k", k=P)

        HALO = CONV_WIDTH - 1

        def mixer_act(act):
            act.wait_ge(cols_psum, 1)
            nc.scalar.activation(cols[:, 0:120], bank[:, 6, 0:120], ACT.Copy)
            nc.scalar.activation(cols[:, 120:160], bank[:, 7, 0:40], ACT.Copy).then_inc(cols_ready, 1)
            for t in range(TT):
                act.wait_ge(xm_in[t // 2], 16)
                if t == TT - 1:
                    act.wait_ge(cols_ready, 1)
                nc.scalar.activation(bank[:, 2 * t:2 * t + 2].rearrange("p a b -> p (a b)"), x_t[:, t], ACT.Square,
                                     accum_out=ms[:, t:t + 1]).then_inc(msq_done, 1)
            act.wait_ge(mrms, 1)
            nc.scalar.activation(mrstd, ms, ACT.Sqrt).then_inc(mrms, 1)

            def ahead(i):
                for gr in panel_granules(i):
                    split_hi(act, gr)

            ahead(0)
            for k in range(KD):
                act.wait_ge(ht_psum, k + 1)
                act.wait_ge(cols_ready, 1)
                nc.scalar.activation(t_hi[:, k], bank[:, k], ACT.Copy, scale=col_nm(k)).then_inc(ht_hi, 1)
            act.wait_ge(dtw_in, 16)
            nc.scalar.activation(u_hi[:, 0, 0:256], dtw_raw.rearrange("p k h -> p (k h)"), ACT.Copy).then_inc(dtw_hi, 1)
            for g in range(NG):
                act.wait_ge(rel_psum, g + 1)
                nc.scalar.activation(rowb[:, g], bank[0:HPG, 5 + g, 0:BR], ACT.Copy).then_inc(rel_copied, 1)
            def dt_copies():
                act.wait_ge(dt_psum, 1)
                nc.scalar.activation(dt_rows, bank[0:NHS, 5], ACT.Copy).then_inc(dt_out, 1)
                act.wait_ge(dt_psum, 2)
                nc.scalar.activation(dt_raw.rearrange("p t h -> p (t h)"), bank[:, 4, 0:TT * NHS], ACT.Copy)\
                    .then_inc(dt_out, 1)

            for g in range(NG):
                for name in ("q", "k", "v"):
                    i = order[name, g]
                    ahead(i + 1)
                    if name == "q" and g == 0:
                        act.wait_ge(dtw_lo, 1)
                    if name == "k" and g == 0:
                        act.wait_ge(bias_saved, 16)
                        act.wait_ge(rel_saved, 16 * NG)
                        act.wait_ge(tok_zeroed, 16)
                    for j in range(4):
                        wait_tile(act, name, g, j)
                        dst = {"q": q_t[g], "k": k_t, "v": v_t}[name][:, j]
                        scale = HEAD_DIM ** -0.5 if name == "q" else 1.0
                        nc.scalar.activation(dst, bank[:, j], ACT.Copy, scale=scale).then_inc(act_out, 1)
                    if name == "q" and g == 0:
                        dt_copies()

                def exponentials(h):
                    n = HPG * g + h
                    act.wait_ge(neg_ready, n + 1)
                    if n >= 2:
                        act.wait_ge(pt_psum, n - 1)
                    for t in range(TT):
                        m = nc.scalar.activation(probs(g, n)[:, t], logits(g, n)[:, t], ACT.Exp,
                                                 bias=nm_t[n % 2][:, t:t + 1], accum_out=d_all[:, g, t, h:h + 1])
                    m.then_inc(p_ready, 1)

                exponentials(0)
                for h in range(HPG):
                    n = HPG * g + h
                    if h < HPG - 1:
                        exponentials(h + 1)
                    if g == NG - 1 and h in (2, 5):
                        split_hi(act, panel_granules(order["xs", 0])[h // 3])
                    act.wait_ge(pt_psum, n + 1)
                    if n:
                        act.wait_ge(u_psum, n)
                    nb = 7 if g == 0 else 4
                    nc.scalar.activation(pturn[:, 0:nb].rearrange("p a b -> p (a b)"),
                                         bank[:, 6:8].rearrange("p a b -> p (a b)")[:, 0:nb * P], ACT.Copy)\
                        .then_inc(pt_out, 1)
            act.wait_ge(row_less, 1)
            nc.scalar.activation(e_row, e_row, ACT.Exp).then_inc(row_exp, 1)
            for hp in range(4):
                act.wait_ge(attn_sum, hp + 1)
                nc.scalar.activation(u_hi[:, hp], q_t[0][:, hp], ACT.Copy).then_inc(attn_hi, 1)

            def conv(g, j):
                n, f, key = 6 * g + j, conv_columns(g, j), conv_key(g, j)
                wait_tile(act, *key)
                if j >= 4:
                    act.wait_ge(xs_psum, 4 * g + j - 3)
                elif g and j < 2:
                    act.wait_ge(diag_psum, TT * (g - 1) + j + 1)
                nc.scalar.activation(conv_t[n % 2], bank[:, conv_bank(*key)], ACT.Identity, scale=col_cw(HALO, f),
                                     bias=col_cb(f)).then_inc(conv_on, 1)
                act.wait_ge(*out_at[key])
                if g and j == 1:
                    act.wait_ge(off_psum, (TT - 1) * g)
                dst = (b_t, c_t)[j] if j < 2 else conv_t[n % 2]
                nc.scalar.activation(dst, conv_t[n % 2], ACT.Silu).then_inc(conv_silu, 1)

            def xs_copy(g, j):
                act.wait_ge(xs_psum, 4 * g + j + 1)
                nc.scalar.activation(xs[:, :, P * j:P * j + P],
                                     bank[:, 4 + j % 2].rearrange("p (c f) -> p c f", c=TT), ACT.Copy).then_inc(xs_out, 1)

            def turned(g, f):
                n = 4 * g + f
                act.wait_ge(yt_psum, n + 1)
                if n >= 2:
                    act.wait_ge(yt_saved[f % 2], 16 * (n // 2))
                nc.scalar.activation(y_turn[f % 2], bank[:, 6 + f % 2], ACT.Copy, scale=col_sn(4 * g + f))\
                    .then_inc(yt_out, 1)

            def z_silu(g, t):
                wait_tile(act, "z", g, t)
                nc.scalar.activation(zs[:, t], bank[:, 6 + t % 2], ACT.Silu).then_inc(act_out, 1)

            def squares(g, c):
                act.wait_ge(y_chunk, TT * g + c + 1)
                nc.scalar.activation(xs[:, c], zs[:, c], ACT.Square, accum_out=gss[:, c:c + 1]).then_inc(gsq_done, 1)

            def decays():
                act.wait_ge(sp_abs, 1)
                nc.scalar.activation(sp[1], sp[0], ACT.Exp, scale=-1.0).then_inc(sp_exp, 1)
                nc.scalar.activation(a_neg, a_neg, ACT.Exp).then_inc(sp_exp, 1)
                act.wait_ge(sp_one, 1)
                nc.scalar.activation(sp[3], sp[2], ACT.Ln).then_inc(sp_ln, 1)

            for g in range(NSG):
                if g == 0:
                    conv(0, 0)
                    conv(0, 1)
                    decays()
                for j in range(4):
                    conv(g, 2 + j)
                    if j == 1:
                        ahead(order["z", g])
                    if g == 0 and j == 1:
                        act.wait_ge(cs_psum, 1)
                        nc.scalar.activation(dec3.rearrange("p a t h -> p (a t h)"), bank[:, 7, 0:3 * TT * NHS],
                                             ACT.Exp).then_inc(cs_exp, 1)
                    if j:
                        xs_copy(g, j - 1)
                    if g:
                        turned(g - 1, j)
                z_silu(g, 0)
                xs_copy(g, 3)
                act.wait_ge(bt_psum, g + 1)
                nc.scalar.activation(b_tok.rearrange("p c n -> p (c n)"), bank[:, 3], ACT.Copy).then_inc(bt_out, 1)
                for c in range(TT):
                    i = TT * g + c
                    act.wait_ge(seg_psum, i + 1)
                    if i >= 2:
                        act.wait_ge(diag_psum, i - 1)
                    nc.scalar.activation(dec[i % 2].rearrange("p h l -> p (h l)"),
                                         bank[:, 4:6].rearrange("p a b -> p (a b)"), ACT.Exp).then_inc(dec_ready, 1)
                    if c < TT - 1:
                        z_silu(g, c + 1)
                    if c == 0:
                        ahead(order["z", g] + 1)
                for c in range(TT - 1):
                    squares(g, c)
                if g < NSG - 1:
                    ahead(order["z", g] + 2)
                    conv(g + 1, 0)
                squares(g, TT - 1)
                act.wait_ge(grms, 2 * g + 1)
                nc.scalar.activation(grstd, gss, ACT.Sqrt).then_inc(grms, 1)
                if g < NSG - 1:
                    conv(g + 1, 1)

            for i in range(4):
                if i < 3:
                    ahead(order["gate", i + 1])
                else:
                    ahead(order["attn", 0])
                    ahead(order["attn", 1])
                if i == 0:
                    for f in range(4):
                        turned(NSG - 1, f)
                for j in range(4):
                    f = 4 * i + j
                    wait_tile(act, "gate", i, j)
                    nc.scalar.activation(gates[:, f // KD, f % KD], bank[:, j], ACT.Sigmoid, bias=col_gb(f))\
                        .then_inc(act_out, 1)
            ahead(order["ssm", 0])
            ahead(order["ssm", 1])

            def rows_back(g, dst, until):
                act.wait_ge(yb_in[g % 3], 16 * (g // 3 + 1))
                act.wait_ge(granule_used, until)
                nc.scalar.activation(dst, y_back[g % 3], ACT.Copy).then_inc(yb_hi, 1)

            rows_back(0, t_hi[:, 0:4], first_of["attn", 0])
            rows_back(1, t_hi[:, 4:8], first_of["attn", 0])
            ahead(order["ssm", 2])
            ahead(order["ssm", 3])
            rows_back(2, u_hi[:], first_of["ssm", 0])
            ahead(order["ssm", 4])
            ahead(order["ssm", 5])
            rows_back(3, t_hi[:, 0:4], first_of["ssm", 2])
            ahead(order["ssm", 6])
            ahead(order["ssm", 7])
            ahead(order["out", 0])
            for f in range(KD):
                if f == 4:
                    act.wait_ge(granule_used, first_of["out", 0])
                act.wait_ge(merged_f, f + 1)
                nc.scalar.activation(t_hi[:, (f + 4) % KD], gates[:, 1, f], ACT.Copy).then_inc(merged_hi, 1)
            ahead(order["out", 1])

        def mixer_pool(pool):
            nc.gpsimd.memset(zero_i, 0).then_inc(zero_set, 1)
            for g in range(NSG):
                hs = slice(HPG * g, HPG * g + HPG)

                def ramps(c):
                    i = TT * g + c
                    if i == 0:
                        pool.wait_ge(a_ready, 1)
                    else:
                        pool.wait_ge(seg_psum, i)
                    nc.gpsimd.tensor_tensor(ramp, bc(tri_le, [(0, HPG), (1, P)]),
                                            bc(a_d[:, c, hs], [(1, HPG), (0, P)]), ALU.mult).then_inc(ramp_ready, 1)

                def state_x(c):
                    n = (TT - 1) * g + c
                    pool.wait_ge(xd_ready, TT * g + c + 1)
                    if n:
                        pool.wait_ge(st_psum, n)
                    nc.gpsimd.tensor_tensor(xdd.rearrange("p (h q) -> p h q", h=HPG),
                                            xd[c].rearrange("p (h q) -> p h q", h=HPG),
                                            bc(dec3[:, 1, c, hs], [(1, HPG), (0, 64)]), ALU.mult).then_inc(xdd_ready, 1)

                ramps(0)
                if g == 0:
                    pool.wait_ge(cs_exp, 1)
                state_x(0)
                for c in range(TT):
                    if c < TT - 1:
                        ramps(c + 1)
                    pool.wait_ge(xd_ready, TT * g + c + 1)
                    if g == 0 and c == 0:
                        pool.wait_ge(dtc_in, 48)
                    x3 = xs[:, c].rearrange("p (h q) -> p h q", h=HPG)
                    nc.gpsimd.tensor_tensor(x3, x3, bc(dskip[:, hs], [(1, HPG), (0, 64)]), ALU.mult)\
                        .then_inc(skip_ready, 1)
                    if c < TT - 2:
                        state_x(c + 1)

        def mixer_dve(dve, link):
            dve.wait_ge(msq_done, TT)
            nc.vector.tensor_scalar(ms, ms, 1.0 / D, EPS, ALU.mult, ALU.add).then_inc(mrms, 1)
            dve.wait_ge(mrms, 2)
            link(nc.vector.reciprocal(mrstd, mrstd))
            for t in range(TT):
                nc.vector.tensor_scalar(x_t[:, t], x_t[:, t], mrstd[:, t:t + 1], None, ALU.mult).then_inc(xn_ready, 1)

            def ahead(i):
                for gr in panel_granules(i):
                    split_lo(dve, gr)

            ahead(0)
            for k in range(KD):
                dve.wait_ge(ht_hi, k + 1)
                nc.vector.scalar_tensor_tensor(out=t_lo[:, k], in0=bank[:, k], scalar=col_nm(k),
                                               in1=t_hi[:, k].bitcast(F32), op0=ALU.mult, op1=ALU.subtract)\
                    .then_inc(ht_lo, 1)
            dve.wait_ge(dtw_hi, 1)
            nc.vector.tensor_tensor(u_lo[:, 0, 0:256], dtw_raw.rearrange("p k h -> p (k h)"),
                                    u_hi[:, 0, 0:256].bitcast(F32), ALU.subtract).then_inc(dtw_lo, 1)
            dve.wait_ge(bias_raw_in, 32)
            for q in range(2):
                link(nc.vector.tensor_copy(bpart[:, q], bfull))
                link(nc.vector.tensor_tensor(bfull, bfull, bpart[:, q], ALU.subtract))
            nc.vector.tensor_copy(bpart[:, 2], bfull).then_inc(bias_split, 5)

            def outputs_back(g, hp):
                dve.wait_ge(u_psum, HPG * g + 2 * hp + 2)
                nc.vector.tensor_copy(group_tokens(q_t[g][:, hp], g), in_tiles(bank[:, hp % 2])).then_inc(u_out, 1)

            for g in range(NG):
                for name in ("q", "k", "v"):
                    ahead(order[name, g] + 1)
                for h in range(HPG):
                    if g == NG - 1 and h in (4, 7):
                        split_lo(dve, panel_granules(order["xs", 0])[(h - 4) // 3])
                    n = HPG * g + h
                    lg = logits(g, n)
                    dve.wait_ge(s_psum, n + 1)
                    dve.wait_ge(bias_in, 16 * (g + 1))
                    if g == 0:
                        nc.vector.memset(lg[:, 0, 0:P], -BIG)
                        nc.vector.tensor_tensor(lg[:, 0, P:], lg[:, 0, P:], bias_t[:, h, P:], ALU.add)
                        nc.vector.tensor_tensor(lg[:, 1:4], lg[:, 1:4], bc(bias_t[:, h], [(0, 3), (1, 2 * P)]),
                                                ALU.add).then_inc(s_out, 1)
                    else:
                        nc.vector.tensor_tensor(lg, lg, bc(bias_t[:, h, 0:P], [(0, TT), (1, P)]), ALU.add)\
                            .then_inc(s_out, 1)
                    dve.wait_ge(s_out, n + 1)
                    link(nc.vector.tensor_reduce(m_all[:, g, :, h], lg, AX.X, ALU.max))
                    if n >= 2:
                        dve.wait_ge(p_ready, n - 1)
                    nc.vector.tensor_scalar(nm_t[n % 2], m_all[:, g, :, h], -1.0, None, ALU.mult).then_inc(neg_ready, 1)
                    if h >= 4 and h % 2 == 0:
                        outputs_back(g, (h - 4) // 2)
                outputs_back(g, 2)
                outputs_back(g, 3)

            for g in range(NG):
                for kind, row in ((0, m_row), (1, d_row)):
                    dve.wait_ge(row_psum, 2 * g + kind + 1)
                    nc.vector.tensor_copy(group_tokens(row[:, g], g), in_tiles(bank[0:HPG, 3 * kind + g]))\
                        .then_inc(row_out, 1)
            dve.wait_ge(row_out, 2 * NG)
            link(nc.vector.tensor_tensor(top_row, m_row[:, 0], m_row[:, 1], ALU.max))
            link(nc.vector.tensor_tensor(top_row, top_row, m_row[:, 2], ALU.max))
            nc.vector.tensor_tensor(e_row, m_row, bc(top_row, [(0, NG), (1, SEQ)]), ALU.subtract).then_inc(row_less, 1)
            dve.wait_ge(row_exp, 1)
            link(nc.vector.tensor_tensor(d_row, d_row, e_row, ALU.mult))
            link(nc.vector.tensor_tensor(z_row, d_row[:, 0], d_row[:, 1], ALU.add))
            link(nc.vector.tensor_tensor(z_row, z_row, d_row[:, 2], ALU.add))
            link(nc.vector.reciprocal(z_row, z_row))
            nc.vector.tensor_tensor(e_row, e_row, bc(z_row, [(0, NG), (1, SEQ)]), ALU.mult).then_inc(share_ready, 1)
            for hp in range(4):
                for g in range(NG):
                    n = NG * hp + g
                    dve.wait_ge(share_psum, n + 1)
                    nc.vector.tensor_tensor(q_t[g][:, hp], q_t[g][:, hp], bank[:, n % 4], ALU.mult)\
                        .then_inc(share_used, 1)
                dve.wait_ge(share_used, NG * hp + NG)
                link(nc.vector.tensor_tensor(q_t[0][:, hp], q_t[0][:, hp], q_t[1][:, hp], ALU.add))
                nc.vector.tensor_tensor(q_t[0][:, hp], q_t[0][:, hp], q_t[2][:, hp], ALU.add).then_inc(attn_sum, 1)
                dve.wait_ge(attn_hi, hp + 1)
                nc.vector.tensor_tensor(u_lo[:, hp], q_t[0][:, hp], u_hi[:, hp].bitcast(F32), ALU.subtract)\
                    .then_inc(attn_lo, 1)

            def conv(g, j):
                n, f, key = 6 * g + j, conv_columns(g, j), conv_key(g, j)
                dve.wait_ge(conv_on, n + 1)
                for back in range(1, CONV_WIDTH):
                    m = nc.vector.scalar_tensor_tensor(
                        out=conv_t[n % 2][:, back:], in0=bank[:, conv_bank(*key), 0:SEQ - back], scalar=col_cw(HALO - back, f),
                        in1=conv_t[n % 2][:, back:], op0=ALU.mult, op1=ALU.add)
                    if back < HALO:
                        link(m)
                m.then_inc(dve_out, 1)

            def heads(ap):
                return ap.rearrange("p (h q) -> p h q", h=HPG)

            def decays():
                dve.wait_ge(dtc_in, 48)
                dve.wait_ge(dt_out, 2)
                link(nc.vector.tensor_tensor(dts, dt_raw, bc(dtb, [(0, TT), (1, NHS)]), ALU.add))
                nc.vector.scalar_tensor_tensor(out=sp[0], in0=dts, scalar=-1.0, in1=dts, op0=ALU.mult, op1=ALU.max)\
                    .then_inc(sp_abs, 1)
                dve.wait_ge(sp_exp, 1)
                nc.vector.tensor_scalar(sp[2], sp[1], 1.0, None, ALU.add).then_inc(sp_one, 1)
                dve.wait_ge(sp_one, 1)
                link(nc.vector.scalar_tensor_tensor(out=sp[0], in0=sp[2], scalar=-1.0, in1=sp[1], op0=ALU.add,
                                                    op1=ALU.subtract))
                dve.wait_ge(sp_ln, 1)
                link(nc.vector.tensor_tensor(sp[3], sp[3], sp[0], ALU.subtract))
                link(nc.vector.scalar_tensor_tensor(out=dts, in0=dts, scalar=0.0, in1=sp[3], op0=ALU.max, op1=ALU.add))
                dve.wait_ge(sp_exp, 2)
                nc.vector.scalar_tensor_tensor(out=a_d, in0=dts, scalar=-1.0, in1=bc(a_neg, [(0, TT), (1, NHS)]),
                                               op0=ALU.mult, op1=ALU.mult).then_inc(a_ready, 1)

            for g in range(NSG):
                hs = slice(HPG * g, HPG * g + HPG)
                if g == 0:
                    conv(0, 0)
                    conv(0, 1)
                    decays()
                for j in range(4):
                    conv(g, 2 + j)
                    if j == 1:
                        ahead(order["z", g])
                dve.wait_ge(xs_out, 4 * g + 4)
                for c in range(TT):
                    nc.vector.tensor_tensor(heads(xd[c]), heads(xs[:, c]), bc(dts[:, c, hs], [(1, HPG), (0, 64)]), ALU.mult)\
                        .then_inc(xd_ready, 1)
                dve.wait_ge(cb_psum, g + 1)
                nc.vector.tensor_tensor(cbm, bank[:, 2].rearrange("p (c l) -> p c l", c=TT),
                                        bc(tri_le, [(0, TT), (1, P)]), ALU.mult).then_inc(cb_out, 1)
                dve.wait_ge(cb_out, g + 1)
                dve.wait_ge(cs_exp, 1)
                for c in range(TT):
                    i = TT * g + c
                    dve.wait_ge(dec_ready, i + 1)
                    nc.vector.tensor_tensor(dec[i % 2], dec[i % 2], bc(cbm[:, c], [(0, HPG), (1, P)]), ALU.mult)\
                        .then_inc(mat_ready, 1)
                    if c == TT - 1 and g < NSG - 1:
                        ahead(order["z", g] + 2)
                    if c:
                        dve.wait_ge(off_psum, 3 * g + c)
                        dve.wait_ge(y_chunk, i)
                        nc.vector.tensor_tensor(heads(y_t), heads(bank[:, 2]), bc(dec3[:, 0, c, hs], [(1, HPG), (0, 64)]),
                                                ALU.mult).then_inc(off_used, 1)
                    if c < TT - 1:
                        if c:
                            link(nc.vector.tensor_tensor(heads(state), heads(state),
                                                         bc(dec3[:, 2, c, hs], [(1, HPG), (0, 64)]), ALU.mult))
                        dve.wait_ge(st_psum, 3 * g + c + 1)
                        if c:
                            nc.vector.tensor_tensor(state, state, bank[:, 3], ALU.add).then_inc(st_used, 1)
                        else:
                            nc.vector.tensor_copy(state, bank[:, 3]).then_inc(st_used, 1)
                    dve.wait_ge(skip_ready, i + 1)
                    if c:
                        dve.wait_ge(off_used, 3 * g + c)
                        nc.vector.tensor_tensor(y_t, y_t, xs[:, c], ALU.add).then_inc(skip_used, 1)
                        if c == TT - 1 and g < NSG - 1:
                            conv(g + 1, 0)
                        dve.wait_ge(skip_used, i + 1)
                        dve.wait_ge(diag_psum, i + 1)
                        link(nc.vector.tensor_tensor(y_t, y_t, bank[:, i % 2], ALU.add))
                    else:
                        if g:
                            dve.wait_ge(y_chunk, i)
                        dve.wait_ge(diag_psum, i + 1)
                        nc.vector.tensor_tensor(y_t, bank[:, i % 2], xs[:, c], ALU.add).then_inc(skip_used, 1)
                        dve.wait_ge(skip_used, i + 1)
                    wait_out(dve, "z", g, c)
                    nc.vector.tensor_tensor(zs[:, c], y_t, zs[:, c], ALU.mult).then_inc(y_chunk, 1)
                    if c == 0:
                        ahead(order["z", g] + 1)
                dve.wait_ge(gsq_done, TT * g + TT)
                nc.vector.tensor_scalar(gss, gss, 1.0 / 512, EPS, ALU.mult, ALU.add).then_inc(grms, 1)
                dve.wait_ge(grms, 2 * g + 2)
                link(nc.vector.reciprocal(grstd, grstd))
                for c in range(TT):
                    nc.vector.tensor_scalar(zs[:, c], zs[:, c], grstd[:, c:c + 1], None, ALU.mult).then_inc(yn_ready, 1)
                if g < NSG - 1:
                    conv(g + 1, 1)

            for i in range(3):
                ahead(order["gate", i + 1])
            ahead(order["attn", 0])
            ahead(order["attn", 1])
            ahead(order["ssm", 0])
            ahead(order["ssm", 1])

            def rows_back(g, hi, lo):
                dve.wait_ge(yb_hi, g + 1)
                nc.vector.tensor_tensor(lo, y_back[g % 3], hi.bitcast(F32), ALU.subtract).then_inc(yb_lo, 1)

            rows_back(0, t_hi[:, 0:4], t_lo[:, 0:4])
            rows_back(1, t_hi[:, 4:8], t_lo[:, 4:8])
            for f in range(KD):
                wait_tile(dve, "attn", f // 4, f % 4)
                wait_out(dve, "gate", f // 4, f % 4)
                nc.vector.tensor_tensor(gates[:, 0, f], gates[:, 0, f], bank[:, f], ALU.mult).then_inc(dve_out, 1)
            ahead(order["ssm", 2])
            ahead(order["ssm", 3])
            rows_back(2, u_hi[:], u_lo[:])
            ahead(order["ssm", 4])
            ahead(order["ssm", 5])
            rows_back(3, t_hi[:, 0:4], t_lo[:, 0:4])
            ahead(order["ssm", 6])
            ahead(order["ssm", 7])
            ahead(order["out", 0])

            def merged_low(f):
                dve.wait_ge(merged_hi, f + 1)
                slot = (f + 4) % KD
                nc.vector.tensor_tensor(t_lo[:, slot], gates[:, 1, f], t_hi[:, slot].bitcast(F32), ALU.subtract)\
                    .then_inc(merged_lo, 1)

            for f in range(KD):
                wait_tile(dve, "ssm", 6 + f // 4, f % 4)
                wait_out(dve, "gate", 2 + f // 4, f % 4)
                nc.vector.tensor_tensor(gates[:, 1, f], gates[:, 1, f], bank[:, f], ALU.mult).then_inc(dve_out, 1)
                wait_out(dve, "ssm", 6 + f // 4, f % 4)
                nc.vector.tensor_tensor(gates[:, 1, f], gates[:, 1, f], gates[:, 0, f], ALU.add).then_inc(merged_f, 1)
                if 2 <= f < 6:
                    merged_low(f - 2)
            for f in range(4, KD):
                merged_low(f)
            ahead(order["out", 1])
            dve.wait_ge(x_in, 16)
            for h in range(2):
                for t in range(TT):
                    wait_tile(dve, "out", h, t)
                    nc.vector.tensor_tensor(resid[:, t, 512 * h:512 * h + 512], resid[:, t, 512 * h:512 * h + 512],
                                            bank[:, 4 * h + t], ALU.add).then_inc(dve_out, 1)

        def mixer_pe(pe):
            pe.wait_ge(const_in, 16)
            pe.wait_ge(cols_in, 80)
            nc.tensor.transpose(bank[:, 6, 0:120], ldrows[0:120], ident[0:120, 0:120])
            nc.tensor.transpose(bank[:, 7, 0:40], ldrows2[0:40], ident[0:40, 0:40]).then_inc(cols_psum, 1)
            pe.wait_ge(cols_ready, 1)
            for t in range(TT):
                pe.wait_ge(xn_ready, t + 1)
                for k in range(KD):
                    m = nc.tensor.transpose(bank[:, k, t * P:(t + 1) * P], x_t[:, t, k * P:(k + 1) * P], ident)
                    if t == TT - 1:
                        m.then_inc(ht_psum, 1)
            pe.wait_ge(ht_lo, KD)
            pe.wait_ge(table_rows_in, 16)
            for g in range(NG):
                nc.tensor.matmul(bank[0:HPG, 5 + g, 0:BR], hotb[:, 3 * BR + HPG * g:3 * BR + HPG * g + HPG],
                                 hotb[:, BR * g:BR * g + BR], start=True, stop=True).then_inc(rel_psum, 1)
            def step_sizes():
                pe.wait_ge(dtw_lo, 1)
                pe.wait_ge(rel_copied, NG)
                for k in range(KD):
                    heads_k = slice(k * NHS, (k + 1) * NHS)
                    m = product(bank[0:NHS, 5], u_hi[:, 0, heads_k], u_lo[:, 0, heads_k], t_hi[:, k], t_lo[:, k],
                                k == 0, k == KD - 1)
                m.then_inc(dt_psum, 1)
                pe.wait_ge(dt_out, 1)
                for t in range(TT):
                    m = nc.tensor.transpose(bank[:, 4, t * NHS:(t + 1) * NHS], dt_rows[:, t * P:(t + 1) * P],
                                            ident[0:NHS, 0:NHS])
                m.then_inc(dt_psum, 1)

            def panel(name, g, one_tile, before=None, after=None, banks=0, bank_of=None):
                i = order[name, g]
                _, _, tiles, granules, _ = panels[i]
                gr = panel_granules(i)
                steps = 4 if name in ("attn", "ssm") else KD
                per = steps // granules
                for j in range(tiles):
                    if before:
                        before(j)
                    for k in range(steps):
                        w = gr[k // per]
                        if j == 0 and k % per == 0:
                            pe.wait_ge(lo_done, w.n + 1)
                        start, stop = k == 0, k == steps - 1
                        if name == "ssm":
                            start, stop = start and g < 2, stop and g >= 6
                        m = product(bank[:, bank_of(j) if bank_of else banks + j], *one_tile(j, k, w, k % per), start, stop)
                        if j == tiles - 1 and k % per == per - 1:
                            m.then_inc(granule_used, 1)
                    if j < tiles - 1:
                        m.then_inc(tile_done, 1)
                    if after:
                        after(j)

            def channels(act_hi, act_lo, width=512):
                def operands(j, k, w, kk):
                    cols_w = slice(width * kk + P * j, width * kk + P * j + P)
                    return whi[:, w.slot, cols_w], wlo[:, w.slot, cols_w], act_hi(k), act_lo(k)
                return operands

            def tokens(act_hi, act_lo):
                def operands(t, k, w, kk):
                    cols_w = slice(512 * kk, 512 * kk + 512)
                    return act_hi(t, k), act_lo(t, k), whi[:, w.slot, cols_w], wlo[:, w.slot, cols_w]
                return operands

            from_h = channels(lambda k: t_hi[:, k], lambda k: t_lo[:, k])

            for g in range(NG):
                def q_banks(j):
                    if g and j == 0:
                        pe.wait_ge(u_out, 4 * g)
                        pe.wait_ge(p_ready, HPG * g)

                panel("q", g, from_h, q_banks)
                if g == 0:
                    step_sizes()
                panel("k", g, from_h, lambda j: wait_out(pe, "q", g, j))
                panel("v", g, tokens(lambda t, k: group_tokens(t_hi[:, k], g, t),
                                     lambda t, k: group_tokens(t_lo[:, k], g, t)),
                      lambda j: wait_out(pe, "k", g, j))

                def scores(h):
                    n, hp, rows = HPG * g + h, h // 2, slice(64 * (h % 2), 64 * (h % 2) + 64)
                    b0 = 4 if h % 2 == 0 else 2
                    if h == 0:
                        wait_out(pe, "v", g, 3)
                        pe.wait_ge(dt_out, 2)
                        if g == 0:
                            pe.wait_ge(rel_copied, NG)
                    if n >= 2:
                        pe.wait_ge(p_ready, n - 1)
                    for t in range(TT):
                        q1 = group_tokens(q_t[g][rows, hp], g, t)
                        if g == 0:
                            lo_k, lo_c = (t - 1) * P, 256 * (t % 2)
                            if t == 0:
                                lo_k, lo_c = 0, P
                            hi_k = (t + 1) * P
                            m = nc.tensor.matmul(bank[:, b0 + t // 2, lo_c:lo_c + hi_k - lo_k], q1,
                                                 k_t[rows, hp, lo_k:hi_k], start=True, stop=True)
                        else:
                            m = nc.tensor.matmul(bank[:, b0, P * t:P * t + P], q1, group_tokens(k_t[rows, hp], g, t),
                                                 start=True, stop=True)
                    m.then_inc(s_psum, 1)

                if g == 0:
                    blocks = [(0, 0, P)] + [(t, t - 1 + a, P * a) for t in range(1, TT) for a in range(2)]
                else:
                    blocks = [(t, t, 0) for t in range(TT)]

                def turn_probs(h):
                    n = HPG * g + h
                    pe.wait_ge(p_ready, n + 1)
                    if n:
                        pe.wait_ge(pt_out, n)
                    pr = probs(g, n)
                    for b, (t, kt, c0) in enumerate(blocks):
                        m = nc.tensor.transpose(bank[:, 6 + b // 4, P * (b % 4):P * (b % 4) + P],
                                                pr[:, t, c0:c0 + P], ident)
                    m.then_inc(pt_psum, 1)

                def values(h):
                    n, hp, r0 = HPG * g + h, h // 2, 64 * (h % 2)
                    if h >= 4 and h % 2 == 0:
                        pe.wait_ge(u_out, 4 * g + hp - 1)
                    pe.wait_ge(pt_out, n + 1)
                    for b, (t, kt, c0) in enumerate(blocks):
                        first = b == 0 or blocks[b - 1][0] != t
                        last = b == len(blocks) - 1 or blocks[b + 1][0] != t
                        m = nc.tensor.matmul(bank[r0:r0 + 64, hp % 2, P * t:P * t + P], v_t[:, kt, 64 * h:64 * h + 64],
                                             pturn[:, b], start=first, stop=last)
                    m.then_inc(u_psum, 1)

                scores(0)
                scores(1)
                for h in range(HPG):
                    turn_probs(h)
                    if h:
                        values(h - 1)
                    if h < HPG - 2:
                        scores(h + 2)
                values(HPG - 1)

            pe.wait_ge(u_out, 4 * NG)
            pe.wait_ge(p_ready, HPG * NG)
            for g in range(NG):
                for kind, src in ((0, m_all), (1, d_all)):
                    for t in range(TT):
                        m = nc.tensor.transpose(bank[0:HPG, 3 * kind + g, P * t:P * t + P], src[:, g, t], ident)
                    m.then_inc(row_psum, 1)
            def bc_panel(g, after=None):
                panel("bc", g, channels(lambda k: t_hi[:, k], lambda k: t_lo[:, k], 256),
                      lambda j: wait_out(pe, "z", g - 1, 2 + j) if g else None, after, banks=6)

            bc_panel(0)
            pe.wait_ge(share_ready, 1)
            for hp in range(4):
                for g in range(NG):
                    n = NG * hp + g
                    if n >= 4:
                        pe.wait_ge(share_used, n - 3)
                    for half in range(2):
                        m = nc.tensor.matmul(bank[64 * half:64 * half + 64, n % 4],
                                             bc(ident[0:HPG, 2 * hp + half:2 * hp + half + 1], [(0, 64)]),
                                             e_row[:, g], start=True, stop=True)
                    m.then_inc(share_psum, 1)
            pe.wait_ge(share_used, 4 * NG)

            def turned(g, f):
                n = 4 * g + f
                if f == 0:
                    pe.wait_ge(yn_ready, TT * g + TT)
                if n >= 2:
                    pe.wait_ge(yt_out, n - 1)
                for c in range(TT):
                    m = nc.tensor.transpose(bank[:, 6 + f % 2, P * c:P * c + P], zs[:, c, P * f:P * f + P], ident)
                m.then_inc(yt_psum, 1)

            for g in range(NSG):
                def x_turn(j):
                    n = 4 * g + j
                    if j < 2 and g:
                        pe.wait_ge(dec_ready, TT * g)
                    if j >= 2:
                        pe.wait_ge(xs_out, n - 1)
                    pe.wait_ge(conv_silu, 6 * g + 3 + j)
                    for c in range(TT):
                        m = nc.tensor.transpose(bank[:, 4 + j % 2, P * c:P * c + P],
                                                conv_t[j % 2][:, P * c:P * c + P], ident)
                    m.then_inc(xs_psum, 1)

                def xs_banks(j):
                    if g and j < 2:
                        pe.wait_ge(y_chunk, TT * g - 1 + j)

                def xs_after(j):
                    if g == 0 and j == 1:
                        pe.wait_ge(a_ready, 1)
                        wait_out(pe, "bc", 0, 1)
                        for q, lhs in enumerate((tri_le, tri_gt, ones)):
                            m = nc.tensor.matmul(bank[:, 7, P * q:P * q + P], lhs, a_d.rearrange("p t h -> p (t h)"),
                                                 start=True, stop=True)
                        m.then_inc(cs_psum, 1)
                    if j:
                        x_turn(j - 1)
                    if g:
                        if j < 2:
                            wait_out(pe, "bc", g, j)
                        turned(g - 1, j)

                panel("xs", g, from_h, xs_banks, xs_after)

                def z_banks(t):
                    if t >= 2:
                        wait_out(pe, "z", g, t - 2)
                    elif g:
                        pe.wait_ge(yt_out, 4 * g - 1 + t)
                    elif t:
                        pe.wait_ge(cs_exp, 1)
                    else:
                        wait_out(pe, "bc", 0, 0)

                def segments(c):
                    i = TT * g + c
                    pe.wait_ge(ramp_ready, i + 1)
                    if c == 0:
                        pe.wait_ge(xs_out, 4 * g + 4)
                    if i:
                        pe.wait_ge(dec_ready, i)
                    for a in range(2):
                        m = nc.tensor.matmul(bank[:, 4 + a], tri_gt,
                                             ramp[:, 4 * a:4 * a + 4].rearrange("p h l -> p (h l)"), start=True, stop=True)
                    m.then_inc(seg_psum, 1)

                def from_state(c):
                    pe.wait_ge(st_used, 3 * g + c)
                    if c > 1:
                        pe.wait_ge(off_used, 3 * g + c - 1)
                    nc.tensor.matmul(bank[:, 2], c_t[:, P * c:P * c + P], state, start=True, stop=True)\
                        .then_inc(off_psum, 1)

                def chunk(c):
                    i = TT * g + c
                    if c < TT - 1:
                        segments(c + 1)
                    if c and not (c == TT - 1 and g < NSG - 1):
                        from_state(c)
                    if c < TT - 1:
                        pe.wait_ge(xdd_ready, 3 * g + c + 1)
                        pe.wait_ge(bt_out, g + 1)
                        nc.tensor.matmul(bank[:, 3], b_tok[:, c], xdd, start=True, stop=True).then_inc(st_psum, 1)
                    pe.wait_ge(mat_ready, i + 1)
                    pe.wait_ge(xd_ready, i + 1)
                    if c >= 2:
                        pe.wait_ge(y_chunk, i - 1)
                    for h in range(HPG):
                        m = nc.tensor.matmul(bank[:, i % 2, 64 * h:64 * h + 64], dec[i % 2][:, h],
                                             xd[c][:, 64 * h:64 * h + 64], start=True, stop=True)
                    m.then_inc(diag_psum, 1)

                def z_after(t):
                    if t:
                        chunk(t - 1)
                        return
                    x_turn(3)
                    for c in range(TT):
                        m = nc.tensor.transpose(bank[:, 3, P * c:P * c + P], b_t[:, P * c:P * c + P], ident)
                    m.then_inc(bt_psum, 1)
                    for c in range(TT):
                        m = nc.tensor.matmul(bank[:, 2, P * c:P * c + P], b_t[:, P * c:P * c + P],
                                             c_t[:, P * c:P * c + P], start=True, stop=True)
                    m.then_inc(cb_psum, 1)
                    segments(0)

                panel("z", g, tokens(lambda t, k: t_hi[:, k, P * t:P * t + P], lambda t, k: t_lo[:, k, P * t:P * t + P]),
                      z_banks, z_after, bank_of=lambda t: 6 + t % 2)
                if g < NSG - 1:
                    bc_panel(g + 1, lambda j: from_state(TT - 1) if j == 0 else None)
                chunk(TT - 1)

            for i in range(4):
                panel("gate", i, from_h,
                      (lambda j: wait_out(pe, "gate", i - 1, j)) if i else (lambda j: pe.wait_ge(y_chunk, TT * NSG)),
                      (lambda j: [turned(NSG - 1, f) for f in range(4)] if j == 0 else None) if i == 0 else None)
            for h in range(2):
                def attn_banks(j):
                    if h == 0:
                        wait_out(pe, "gate", 3, j)
                    elif j == 0:
                        pe.wait_ge(yt_out, 4 * NSG)
                panel("attn", h, channels(lambda k: u_hi[:, k], lambda k: u_lo[:, k]), attn_banks, banks=4 * h)
            for g in range(NSG):
                pe.wait_ge(yb_lo, g + 1)
                hi, lo, k0 = ((t_hi, t_lo, 0), (t_hi, t_lo, 4), (u_hi, u_lo, 0), (t_hi, t_lo, 0))[g]
                for h in range(2):
                    panel("ssm", 2 * g + h, channels(lambda k: hi[:, k0 + k], lambda k: lo[:, k0 + k]),
                          (lambda j: wait_out(pe, "attn", h, j)) if g == 0 else None, banks=4 * h)

            def merged_rows(t, k):
                if t == 0:
                    pe.wait_ge(merged_lo, k + 1)
                return t_hi[:, (k + 4) % KD, P * t:P * t + P]

            for h in range(2):
                panel("out", h, tokens(merged_rows, lambda t, k: t_lo[:, (k + 4) % KD, P * t:P * t + P]),
                      lambda j: wait_out(pe, "ssm", 6 + h, j), banks=4 * h)

        block = ctx.enter_context(nc.Block())

        @block.sync
        def _(sp):
            mixer_loads(sp)
            sp.wait_ge(merged_lo, KD)
            sp.dma_start(wffn, norm_ffn.broadcast_to([P, D])).then_inc(norm_in, 16)
            sp.dma_start(rw, router_w.rearrange("a (k p) e -> p (a k) e", p=P)).then_inc(router_in, 16)
            sp.dma_start(rb, router_b.broadcast_to([P, NE])).then_inc(router_in, 16)
            sp.dma_start(late, consts[:, C_LT:C_ALL]).then_inc(late_in, 16)

            def hidden(g, e, c, half):
                load(sp, g, w1_v[e, :, 4 * half:4 * half + 4, 512 * c:512 * c + 512], 4)

            def run(passes):
                if later(passes):
                    sp.wait_ge(comb_used, passes * TT * TOPK)
                g = first_granules(passes)
                for s in range(3):
                    hidden(g[2 * s], 0, s, 0)
                    hidden(g[2 * s + 1], 0, s, 1)

                def body(e, c, last):
                    g = step_granules(c, passes, e, last)
                    load(sp, g[0], w2_v[e, :, 2 * c:2 * c + 2, :], 2)
                    if len(g) == 3:
                        ahead = e if c == 0 else e + 1
                        hidden(g[1], ahead, (c + 3) % 4, 0)
                        hidden(g[2], ahead, (c + 3) % 4, 1)

                expert_loop(sp, body, passes)

            over_passes(sp, run)
            sp.wait_ge(h2_ready, TT)
            sp.dma_start(wfin, norm_final.unsqueeze(0).broadcast_to([P, D])).then_inc(fin_in, 16)
            for t in range(TT):
                sp.wait_ge(out_ready, t + 1)
                sp.dma_start(out_rows[:, t], resid[:, t]).then_inc(out_saved, 16)
            sp.wait_ge(out_saved, 16 * TT)

        @block.gpsimd
        def _(pool):
            mixer_pool(pool)
            pool.wait_ge(h2_ready, TT)
            nc.gpsimd.iota(tokc, [[P, TT]], base=0, channel_multiplier=1).then_inc(ids_set, 1)
            pool.wait_ge(ids_set, 1)
            pool.wait_ge(tok_zeroed, 16)
            pool.wait_ge(places_ready, 1)
            for j in range(TT * TOPK):
                pool.indirect_dma_start(tok_d, bass.IndirectOffsetOnAxis(place_i[:, j:j + 1], 0),
                                        tokc[:, j // TOPK:j // TOPK + 1], None).then_inc(tok_saved, 16)
            pool.wait_ge(tok_saved, 16 * TT * TOPK)
            pool.dma_start(table, tok_d.rearrange("(b p e) a -> p b (e a)", b=NPASS, p=P)).then_inc(table_in, 16)
            pool.wait_ge(table_in, 16)
            pool.wait_ge(h2_saved, 16)
            pool.wait_ge(bias_saved, 16)

            def gather(passes, e, first):
                n = passes * NE + e
                if not first:
                    pool.wait_ge(xg_in, n * 16)
                    pool.wait_ge(xt_psum, n)
                nc.gpsimd.tensor_copy(idx, table[:, passes, bass.ds(e, 1)])
                pool.drain()
                pool.indirect_dma_start(xg.rearrange("p k s -> p (k s)"), None, h2_d,
                                        bass.IndirectOffsetOnAxis(idx, 0)).then_inc(xg_in, 16)

            def run(passes):
                gather(passes, 0, not later(passes))
                with pool.Fori(1, NE) as e:
                    gather(passes, e, False)
                pool.wait_ge(y_saved, (passes * NE + NE + 1) * 16)
                for j in range(TT * TOPK):
                    if j >= 8:
                        pool.wait_ge(comb_used, passes * TT * TOPK + j - 7)
                    pool.indirect_dma_start(raw[:, (j % 8) // 2, 1024 * (j % 2):1024 * (j % 2) + 1024], None, y_d,
                                            bass.IndirectOffsetOnAxis(slot_i[:, j:j + 1], 0))\
                        .then_inc(comb_in[j % 8], 16)

            over_passes(pool, run)

        @block.scalar
        def _(act):
            act.sem_inc(y_copied, 1)
            act.sem_inc(y_saved, 16)
            mixer_act(act)
            for t in range(TT):
                wait_out(act, "out", 1, t)
                nc.scalar.activation(bank[:, 2 * t:2 * t + 2].rearrange("p a b -> p (a b)"), resid[:, t], ACT.Square,
                                     accum_out=ss[:, t:t + 1]).then_inc(sq_done, 1)
            act.wait_ge(rms_ready, 1)
            nc.scalar.activation(rstd, ss, ACT.Sqrt).then_inc(rms_ready, 1)
            act.wait_ge(h2_ready, TT)
            act.dma_start(h2_rows, h2).then_inc(h2_saved, 16)
            for k in range(KD):
                act.wait_ge(h2t_psum, k + 1)
                nc.scalar.activation(h2t[:, k], bank[:, k], ACT.Copy).then_inc(h2t_copied, 1)
            act.wait_ge(top_found, 1)
            nc.scalar.activation(wk, wk, ACT.Exp).then_inc(exp_done, 1)

            def sigmoid(n):
                act.wait_ge(glu_ready, n + 1)
                nc.scalar.activation(sig, glu, ACT.Sigmoid, scale=1.702).then_inc(sig_done, 1)

            def turn_hi(n, c):
                act.wait_ge(at_psum, n + 1)
                nc.scalar.activation(u_hi[:, c % 2, 0:256], bank[:, 6 + c % 2, 0:256], ACT.Copy).then_inc(at_hi, 1)

            def rows_hi(n):
                act.wait_ge(xt_psum, n + 1)
                nc.scalar.activation(t_hi[:, 0:2, :].rearrange("p a b -> p (a b)"),
                                     bank[:, 4:6].rearrange("p a b -> p (a b)"), ACT.Copy).then_inc(xt_hi, 1)

            def bias_half(n, e, half):
                act.dma_start(bias1[half], bias_d[e, :, 1024 * half:1024 * half + 1024]).then_inc(bias1_in[half], 16)

            def bias_out(n, e):
                act.dma_start(bias2, bias_d[e, :, HID:3072]).then_inc(bias2_in, 16)

            def run(passes):
                base = passes * STEPS
                g = first_granules(passes)
                for i in range(4):
                    split_hi(act, g[i])
                if not later(passes):
                    act.wait_ge(bias_saved, 16)
                    act.wait_ge(h2_saved, 16)
                    act.wait_ge(places_ready, 2)
                bias_half(passes * NE, 0, 0)
                bias_half(passes * NE, 0, 1)
                bias_out(passes * NE, 0)
                rows_hi(passes * NE)
                sigmoid(base)
                split_hi(act, g[4])
                split_hi(act, g[5])
                turn_hi(base, 0)

                def begin(n, c, e, last):
                    g = step_granules(c, passes, e, last)
                    split_hi(act, g[0])
                    if not (last and c == 3):
                        sigmoid(n + 1)
                    if len(g) > 1:
                        split_hi(act, g[1])

                begin(base, 0, 0, False)

                def body(e, c, last):
                    n = e * 4 + base + c
                    g = step_granules(c, passes, e, last)
                    if len(g) > 1:
                        split_hi(act, g[2])
                    if not (last and c == 3):
                        turn_hi(n + 1, (c + 1) % 2)
                        if c == 1 and not last:
                            act.wait_ge(h_done, e * 4 + base + 4)
                            rows_hi(e + passes * NE + 1)
                        if c < 3:
                            begin(n + 1, c + 1, e, last)
                        else:
                            begin(n + 1, 0, e + 1, False)
                    if c == 0 and not last:
                        bias_half(0, e + 1, 0)
                    if c == 1 and not last:
                        bias_half(0, e + 1, 1)
                    if c == 3:
                        m = e + passes * NE
                        act.wait_ge(y_done, m + 1)
                        if not last:
                            bias_out(0, e + 1)
                        act.wait_ge(y_saved, m * 16 + 16)
                        nc.scalar.activation(ysb, bank[:, 2:4].rearrange("p a b -> p (a b)"), ACT.Copy)\
                            .then_inc(y_copied, 1)
                        act.wait_ge(y_copied, m + 2)
                        act.dma_start(y_rows[e], ysb).then_inc(y_saved, 16)

                expert_loop(act, body, passes)

            over_passes(act, run)
            more = act.value_load(flag_i[0:1, 0:1], min_val=0, max_val=SEQ)
            with act.If(more > CAP):
                act.wait_ge(comb_used, NPASS * TT * TOPK)
            for t in range(TT):
                act.wait_ge(comb_used, TOPK * (t + 1))
                nc.scalar.activation(bank[:, 2 * t:2 * t + 2].rearrange("p a b -> p (a b)"), resid[:, t], ACT.Square,
                                     accum_out=ss2[:, t:t + 1]).then_inc(sq2_done, 1)
            act.wait_ge(rms2_ready, 1)
            nc.scalar.activation(rstd2, ss2, ACT.Sqrt).then_inc(rms2_ready, 1)

        @block.vector
        def _(dve):
            link = Tally(dve, dve_own)
            mixer_dve(dve, link)
            nc.vector.memset(one3, 1.0).then_inc(one3_set, 1)
            dve.wait_ge(sq_done, TT)
            nc.vector.tensor_scalar(ss, ss, 1.0 / D, EPS, ALU.mult, ALU.add).then_inc(rms_ready, 1)
            dve.wait_ge(rms_ready, 2)
            link(nc.vector.reciprocal(rstd, rstd))
            dve.wait_ge(norm_in, 16)
            for t in range(TT):
                nc.vector.scalar_tensor_tensor(out=h2[:, t], in0=resid[:, t], scalar=rstd[:, t:t + 1], in1=wffn,
                                               op0=ALU.mult, op1=ALU.mult).then_inc(h2_ready, 1)
            dve.wait_ge(logit_psum, 1)
            dve.wait_ge(router_in, 32)
            link(nc.vector.tensor_tensor(logit, bank[:, 0:TT, 0:NE],
                                         bc(rb, [(0, TT), (1, NE)]), ALU.add))
            for t in range(TT):
                link(nc.vector.max(mx8[:, t], logit[:, t]))
                link(nc.vector.max_index(ix8[:, t], mx8[:, t], logit[:, t]))
            nc.vector.tensor_tensor(wk, mx8[:, :, 0:TOPK], bc(mx8, [(8, TT), (0, TOPK)]), ALU.subtract)\
                .then_inc(top_found, 1)
            link(nc.vector.tensor_copy(ixf, ix8[:, :, 0:TOPK]))
            dve.wait_ge(late_in, 16)
            link(nc.vector.tensor_tensor(hot, bc(iota, [(0, TT * TOPK), (1, NE)]),
                                         bc(ixf, [(1, TT * TOPK), (0, NE)]), ALU.is_equal))
            nc.vector.tensor_reduce(mask, bc(hot, [(TOPK * NE, TT), (1, NE), (NE, TOPK)]), AX.X,
                                    ALU.add).then_inc(mask_ready, 1)
            dve.wait_ge(exp_done, 1)
            link(nc.vector.tensor_reduce(wsum, wk, AX.X, ALU.add))
            link(nc.vector.reciprocal(wrec, wsum))
            link(nc.vector.tensor_tensor(wk, wk, bc(wrec, [(1, TT), (0, TOPK)]), ALU.mult))
            dve.wait_ge(rank_psum, 1)
            link(nc.vector.tensor_tensor(hotr.rearrange("p (t k) e -> p t k e", t=TT),
                                         hot.rearrange("p (t k) e -> p t k e", t=TT),
                                         bc(bank[:, 1, 0:TT * NE], [(NE, TT), (0, TOPK), (1, NE)]), ALU.mult))
            link(nc.vector.tensor_reduce(rk[:, 0], hotr, AX.X, ALU.add))
            link(nc.vector.tensor_scalar(rk[:, 1], rk[:, 0], float(CAP), None, ALU.is_ge))
            for b in range(2, NPASS):
                link(nc.vector.scalar_tensor_tensor(out=rk[:, 1], in0=rk[:, 0], scalar=float(CAP * b), in1=rk[:, 1],
                                                    op0=ALU.is_ge, op1=ALU.add))
            ixf_flat = ixf.rearrange("p t k -> p (t k)")
            link(nc.vector.scalar_tensor_tensor(out=rk[:, 2], in0=rk[:, 1], scalar=-float(CAP), in1=rk[:, 0],
                                                op0=ALU.mult, op1=ALU.add))
            link(nc.vector.scalar_tensor_tensor(out=rk[:, 3], in0=rk[:, 2], scalar=float(NE), in1=ixf_flat,
                                                op0=ALU.mult, op1=ALU.add))
            link(nc.vector.scalar_tensor_tensor(out=addr[:, 0], in0=rk[:, 1], scalar=float(NE * P), in1=rk[:, 3],
                                                op0=ALU.mult, op1=ALU.add))
            nc.vector.tensor_copy(place_i, addr[:, 0]).then_inc(places_ready, 1)
            link(nc.vector.scalar_tensor_tensor(out=addr[:, 1], in0=ixf_flat, scalar=float(P), in1=rk[:, 2],
                                                op0=ALU.mult, op1=ALU.add))
            for b in range(NPASS):
                link(nc.vector.scalar_tensor_tensor(out=wk_pass[:, b], in0=rk[:, 1], scalar=float(b),
                                                    in1=wk.rearrange("p t k -> p (t k)"), op0=ALU.is_equal,
                                                    op1=ALU.mult))
            nc.vector.tensor_copy(slot_i, addr[:, 1]).then_inc(places_ready, 1)
            dve.wait_ge(rank_psum, 2)
            link(nc.vector.tensor_reduce(longest[:, 0:1], bank[:, 2, 0:NE], AX.X, ALU.max))
            nc.vector.tensor_copy(flag_i, longest[:, 0:1]).then_inc(flag_ready, 1)

            def gate(n, c, between=None):
                hid = bank[:, c % 2].rearrange("p (n two) -> p two n", two=2)
                dve.wait_ge(h_done, n + 1)
                nc.vector.tensor_scalar(glu, hid[:, 0], 7.0, None, ALU.min).then_inc(glu_ready, 1)
                nc.vector.tensor_scalar(lin, hid[:, 1], 7.0, -7.0, ALU.min, ALU.max).then_inc(lin_ready, 1)
                if between:
                    split_lo(dve, between)
                dve.wait_ge(lin_ready, n + 1)
                dve.wait_ge(sig_done, n + 1)
                nc.vector.scalar_tensor_tensor(out=prod, in0=lin, scalar=1.0, in1=sig, op0=ALU.add, op1=ALU.mult)\
                    .then_inc(prod_ready, 1)
                dve.wait_ge(prod_ready, n + 1)
                nc.vector.tensor_tensor(act_t[c % 2], prod, glu, ALU.mult).then_inc(act_ready, 1)

            def turn_lo(n, c):
                dve.wait_ge(at_hi, n + 1)
                nc.vector.tensor_tensor(u_lo[:, c % 2, 0:256], bank[:, 6 + c % 2, 0:256],
                                        u_hi[:, c % 2, 0:256].bitcast(F32), ALU.subtract).then_inc(at_lo, 1)

            def rows_lo(n):
                dve.wait_ge(xt_hi, n + 1)
                nc.vector.tensor_tensor(t_lo[:, 0:2, :].rearrange("p a b -> p (a b)"),
                                        bank[:, 4:6].rearrange("p a b -> p (a b)"),
                                        t_hi[:, 0:2, :].rearrange("p a b -> p (a b)").bitcast(F32),
                                        ALU.subtract).then_inc(xt_lo, 1)

            def run(passes):
                base = passes * STEPS
                g = first_granules(passes)
                for i in range(4):
                    split_lo(dve, g[i])
                rows_lo(passes * NE)
                gate(base, 0)
                split_lo(dve, g[4])
                split_lo(dve, g[5])
                turn_lo(base, 0)

                def body(e, c, last):
                    n = e * 4 + base + c
                    g = step_granules(c, passes, e, last)
                    if last and c == 3:
                        split_lo(dve, g[0])
                    else:
                        gate(n + 1, (c + 1) % 2, g[0])
                    for granule in g[1:]:
                        split_lo(dve, granule)
                    if not (last and c == 3):
                        turn_lo(n + 1, (c + 1) % 2)
                    if c == 1 and not last:
                        rows_lo(e + passes * NE + 1)

                expert_loop(dve, body, passes)
                for j in range(TT * TOPK):
                    t = j // TOPK
                    done = passes * TT * TOPK + j
                    dve.wait_ge(comb_in[j % 8], (passes * 2 + j // 8 + 1) * 16)
                    if j or later(passes):
                        dve.wait_ge(comb_used, done)
                    nc.vector.scalar_tensor_tensor(
                        out=resid[:, t], in0=raw[:, (j % 8) // 2, 1024 * (j % 2):1024 * (j % 2) + 1024],
                        scalar=wk_pass[:, passes, j:j + 1], in1=resid[:, t], op0=ALU.mult, op1=ALU.add)\
                        .then_inc(comb_used, 1)

            over_passes(dve, run)
            dve.wait_ge(sq2_done, TT)
            nc.vector.tensor_scalar(ss2, ss2, 1.0 / D, EPS, ALU.mult, ALU.add).then_inc(rms2_ready, 1)
            dve.wait_ge(rms2_ready, 2)
            link(nc.vector.reciprocal(rstd2, rstd2))
            dve.wait_ge(fin_in, 16)
            for t in range(TT):
                nc.vector.scalar_tensor_tensor(out=resid[:, t], in0=resid[:, t], scalar=rstd2[:, t:t + 1],
                                               in1=wfin, op0=ALU.mult, op1=ALU.mult).then_inc(out_ready, 1)

        @block.tensor
        def _(pe):
            mixer_pe(pe)
            for k in range(KD):
                for t in range(TT):
                    if k == 0:
                        pe.wait_ge(h2_ready, t + 1)
                    m = nc.tensor.transpose(bank[:, k, t * P:(t + 1) * P], h2[:, t, k * P:(k + 1) * P], ident)
                m.then_inc(h2t_psum, 1)
            pe.wait_ge(router_in, 32)
            for k in range(KD):
                for t in range(TT):
                    pe.wait_ge(h2t_copied, max(k, t) + 1)
                    m = nc.tensor.matmul(bank[:, t, 0:NE], h2t[:, k, t * P:(t + 1) * P], rw[:, k],
                                         start=(k == 0), stop=(k == KD - 1))
            m.then_inc(logit_psum, 1)
            pe.wait_ge(mask_ready, 1)
            pe.wait_ge(late_in, 16)
            masks = mask.rearrange("p t e -> p (t e)")
            nc.tensor.matmul(bank[:, 1, 0:TT * NE], tri_lt, masks, start=True, stop=False)
            for j in range(TT - 1):
                m = nc.tensor.matmul(bank[:, 1, (j + 1) * NE:TT * NE], ones, bc(mask[:, j], [(0, TT - 1 - j), (1, NE)]),
                                     start=False, stop=(j == TT - 2))
            m.then_inc(rank_psum, 1)
            for t in range(TT):
                m = nc.tensor.matmul(bank[:, 2, 0:NE], ones, mask[:, t], start=(t == 0), stop=(t == TT - 1))
            m.then_inc(rank_psum, 1)

            def rows(n):
                pe.wait_ge(xg_in, n * 16 + 16)
                if not (isinstance(n, int) and n == 0):
                    pe.wait_ge(xt_lo, n)
                for k in range(KD):
                    m = nc.tensor.transpose(bank[:, 4 + k // 4, (k % 4) * P:(k % 4 + 1) * P], xg[:, k], ident)
                m.then_inc(xt_psum, 1)

            def hidden(g0, g1, c, n, expert):
                hid = bank[:, c % 2]
                if not (isinstance(n, int) and n < 2):
                    pe.wait_ge(act_ready, n - 1)
                for k in range(KD):
                    g = (g0, g1)[k // 4]
                    if k % 4 == 0:
                        pe.wait_ge(lo_done, g.n + 1)
                    cols = slice(512 * (k % 4), 512 * (k % 4) + 512)
                    rows_k = slice(k * P % 512, k * P % 512 + P)
                    m = product(hid, t_hi[:, k // 4, rows_k], t_lo[:, k // 4, rows_k], whi[:, g.slot, cols],
                                wlo[:, g.slot, cols], k == 0, False)
                    if k % 4 == 3:
                        m.then_inc(granule_used, 1)
                pe.wait_ge(bias1_in[c // 2], expert * 16 + 16)
                nc.tensor.matmul(hid, one3, bias1[c // 2][:, 512 * (c % 2):512 * (c % 2) + 512],
                                 start=False, stop=True).then_inc(h_done, 1)

            def turn(n, c):
                pe.wait_ge(act_ready, n + 1)
                for j in range(2):
                    m = nc.tensor.transpose(bank[:, 6 + c % 2, j * P:(j + 1) * P], act_t[c % 2][:, j * P:(j + 1) * P],
                                            ident)
                m.then_inc(at_psum, 1)

            def outputs(g, n, c, expert):
                pe.wait_ge(at_lo, n + 1)
                if c == 0:
                    pe.wait_ge(y_copied, expert + 1)
                pe.wait_ge(lo_done, g.n + 1)
                for j in range(2):
                    for h in range(2):
                        cols = slice(1024 * j + 512 * h, 1024 * j + 512 * h + 512)
                        m = product(bank[:, 2 + h], u_hi[:, c % 2, j * P:(j + 1) * P],
                                    u_lo[:, c % 2, j * P:(j + 1) * P], whi[:, g.slot, cols], wlo[:, g.slot, cols],
                                    c == 0 and j == 0, False)
                m.then_inc(granule_used, 1)
                if c == 3:
                    pe.wait_ge(bias2_in, expert * 16 + 16)
                    for h in range(2):
                        m = nc.tensor.matmul(bank[:, 2 + h], one3, bias2[:, 512 * h:512 * h + 512], start=False,
                                             stop=True)
                    m.then_inc(y_done, 1)

            def run(passes):
                base = passes * STEPS
                g = first_granules(passes)
                rows(passes * NE)
                pe.wait_ge(one3_set, 1)
                pe.wait_ge(xt_lo, passes * NE + 1)
                hidden(g[0], g[1], 0, base, passes * NE)
                hidden(g[2], g[3], 1, base + 1, passes * NE)
                turn(base, 0)

                def body(e, c, last):
                    n = e * 4 + base + c
                    expert = e + passes * NE
                    if c == 1 and not last:
                        rows(expert + 1)
                    if not (last and c >= 2):
                        first = MIX_GRANULES + 3 * c + 4
                        ga, gb = ((Granule(first, passes, e), Granule(first + 1, passes, e)) if not last else
                                  (Granule(first + 12 * (NE - 1), passes), Granule(first + 12 * (NE - 1) + 1, passes)))
                        if c == 2:
                            pe.wait_ge(xt_lo, expert + 2)
                        hidden(ga, gb, (c + 2) % 4, n + 2, expert if c < 2 else expert + 1)
                    if not (last and c == 3):
                        turn(n + 1, (c + 1) % 2)
                    outputs(step_granules(c, passes, e, last)[0], n, c, expert)

                expert_loop(pe, body, passes)

            over_passes(pe, run)




_INS = ['x', 'w_in', 'rel_bias', 'w_branch_attn', 'conv_w', 'conv_b', 'dt_bias', 'a_log', 'd_skip', 'ssm_norm_w',
        'w_branch_ssm', 'gate_bias', 'w_out', 'norm_mix', 'norm_ffn', 'router_w', 'router_b', 'w1', 'b1', 'w2', 'b2',
        'norm_final']
_OUTS = [((1, SEQ, D), 'float32')]


def constants():
    import numpy as np
    p, f = np.arange(P)[:, None], np.arange(P)[None, :]
    return np.concatenate([p == f, p <= f, p > f, np.ones((P, P)), p < f, np.broadcast_to(np.arange(NE), (P, NE))],
                          axis=1).astype(np.float32)


def bucket_rows():
    import math
    import numpy as np
    hot = np.zeros((NBK + 1, 3 * BR + NH_A), np.float32)
    for g, (window, dilation) in enumerate(GROUPS):
        for j in range(BR):
            delta = 255 - j
            if g == 2:
                valid, dist = delta >= 0 and delta % 4 == 0, delta // 4
            else:
                valid, dist = 0 <= delta <= window // dilation, delta
            if not valid:
                hot[NBK, g * BR + j] = -BIG
                continue
            dist *= dilation
            half = NBK // 2
            large = half + int(np.float32(np.log(np.float32(max(dist, half) / half)) / np.float32(
                math.log(MAX_DIST / half)) * np.float32(NBK - half)))
            hot[dist if dist < half else min(large, NBK - 1), g * BR + j] = 1.0
    hot[NBK, 3 * BR:] = 1.0
    return hot


def kernel(**inputs):
    import numpy as _np
    import concourse.bacc as _bacc
    from concourse import mybir as _mybir
    from concourse.bass_utils import run_bass_kernel_spmd as _run

    nc = _bacc.Bacc("TRN2", target_bir_lowering=False, num_devices=1)
    arrays, args = {}, []
    given = [(name, inputs[name]) for name in _INS] + [("consts", constants()), ("buckets", bucket_rows())]
    for name, a in given:
        a = _np.ascontiguousarray(a)
        arrays[f"in_{name}_dram"] = a
        args.append(nc.dram_tensor(f"in_{name}_dram", a.shape, _mybir.dt.from_np(a.dtype), kind="ExternalInput").ap())
    for i, (shape, dtype) in enumerate(_OUTS):
        dt = _mybir.dt.from_np(_np.dtype(dtype))
        args.append(nc.dram_tensor(f"out_{i}_dram", shape, dt, kind="ExternalOutput").ap())
    build(nc, *args)
    r = _run(nc, [arrays], core_ids=[0])
    got = tuple(r.results[0][f"out_{i}_dram"] for i in range(len(_OUTS)))
    return got[0]
```
